# Optimizing a Trainium2 kernel written in Bass

```python
import jax, jax.numpy as jnp
from jax import lax
import numpy as np

D_MODEL = 1024
BATCH = 1
SEQ = 128
DEPTH = 1
DEC_BATCH = 1
DEC_SEQ = 1024
PAST_LEN = 128

GRID_W = 64
CONV_WIDTH = 1024
HGRN_HEADS = 8
HGRN_DK = 128
HGRN_DV = 128
HGRN_KW = HGRN_HEADS * HGRN_DK
HGRN_VW = HGRN_HEADS * HGRN_DV
CHUNK = 32
N_EXPERTS = 16
EC_CAPACITY_FACTOR = 2
D_EXPERT = 1024
EPS = 1e-6
PROJ_WIDTHS = (CONV_WIDTH, CONV_WIDTH, CONV_WIDTH, HGRN_KW, HGRN_KW, HGRN_KW,
               HGRN_VW, HGRN_VW, D_MODEL, D_MODEL)
PROJ_TOTAL = sum(PROJ_WIDTHS)

kernel_name = "hybrid_diffusion_conv_hgrn2_ec_moe_step"

def rmsnorm(x, g):
    xf = x.astype(jnp.float32)
    y = xf * lax.rsqrt(jnp.mean(xf * xf, axis=-1, keepdims=True) + EPS)
    return (y * g.astype(jnp.float32)).astype(x.dtype)

def split_proj(p):
    offs, acc = [], 0
    for w in PROJ_WIDTHS[:-1]:
        acc += w
        offs.append(acc)
    return jnp.split(p, offs, axis=-1)

def short_conv(u, w, b, row_w):
    B, T, Ch = u.shape
    ur = u.reshape(B, T // row_w, row_w, Ch)
    up = jnp.pad(ur, ((0, 0), (0, 0), (1, 1), (0, 0)))
    y = up[:, :, :-2] * w[0] + up[:, :, 1:-1] * w[1] + up[:, :, 2:] * w[2] + b
    return y.reshape(B, T, Ch)

def hgrn2_scan(q, logf, v, s0):
    B, T, H, K = q.shape
    N = T // CHUNK
    k = -jnp.expm1(logf)
    causal = jnp.tril(jnp.ones((CHUNK, CHUNK), dtype=bool))[None, :, :, None, None]

    def to_chunks(a):
        return jnp.moveaxis(a.reshape(B, N, CHUNK, H, a.shape[-1]), 1, 0)

    def step(S, inp):
        qc, lc, kc, vc = inp
        bcum = jnp.cumsum(lc, axis=1)
        o_inter = jnp.einsum('bchk,bhkv->bchv', qc * jnp.exp(bcum), S)
        diff = bcum[:, :, None] - bcum[:, None, :]
        decay = jnp.exp(jnp.where(causal, diff, -jnp.inf))
        attn = jnp.einsum('btshk,bshk->bhts', qc[:, :, None] * decay, kc)
        o_intra = jnp.einsum('bhts,bshv->bthv', attn, vc)
        blast = bcum[:, -1]
        S_new = jnp.exp(blast)[..., None] * S + jnp.einsum(
            'bshk,bshv->bhkv', kc * jnp.exp(blast[:, None] - bcum), vc)
        return S_new, o_inter + o_intra

    S, o = lax.scan(step, s0, (to_chunks(q), to_chunks(logf), to_chunks(k), to_chunks(v)))
    o = jnp.moveaxis(o, 0, 1).reshape(B, T, H, v.shape[-1])
    return o, S

def hgrn2_branch(q_raw, zf, zb, i_raw, g_raw, lb, onorm, s0):
    B, T, _ = q_raw.shape
    f32 = jnp.float32
    q = jax.nn.silu(q_raw.astype(f32)).reshape(B, T, HGRN_HEADS, HGRN_DK)
    v = i_raw.astype(f32).reshape(B, T, HGRN_HEADS, HGRN_DV)
    logf_f = jnp.log(lb[0] + (1.0 - lb[0]) * jax.nn.sigmoid(zf.astype(f32)))
    logf_b = jnp.log(lb[1] + (1.0 - lb[1]) * jax.nn.sigmoid(zb.astype(f32)))
    logf_f = logf_f.reshape(B, T, HGRN_HEADS, HGRN_DK)
    logf_b = logf_b.reshape(B, T, HGRN_HEADS, HGRN_DK)
    s0 = s0.astype(f32)
    o_f, S_f = hgrn2_scan(q, logf_f, v, s0[:, 0])
    o_b, S_b = hgrn2_scan(q[:, ::-1], logf_b[:, ::-1], v[:, ::-1], s0[:, 1])
    o = o_f + o_b[:, ::-1]
    o = o * lax.rsqrt(jnp.mean(o * o, axis=-1, keepdims=True) + EPS)
    o = o * onorm.astype(f32).reshape(HGRN_HEADS, HGRN_DV)
    o = o * jax.nn.silu(g_raw.astype(f32)).reshape(B, T, HGRN_HEADS, HGRN_DV)
    return o.reshape(B, T, HGRN_VW), jnp.stack([S_f, S_b], axis=1)

def expert_choice_ffn(h, w_router, w_g, w_u, w_d):
    B, T, D = h.shape
    cap = EC_CAPACITY_FACTOR * T // N_EXPERTS
    aff = jax.nn.softmax(jnp.einsum('btd,de->bte', h.astype(jnp.float32),
                                    w_router.astype(jnp.float32)), axis=-1)
    top_w, top_idx = lax.top_k(jnp.swapaxes(aff, 1, 2), cap)
    bidx = jnp.arange(B)[:, None, None]
    xs = h[bidx, top_idx]
    hid = jax.nn.silu(jnp.einsum('becd,edf->becf', xs, w_g)) * jnp.einsum('becd,edf->becf', xs, w_u)
    ys = jnp.einsum('becf,efd->becd', hid, w_d) * top_w[..., None].astype(h.dtype)
    return jnp.zeros_like(h).at[bidx, top_idx].add(ys.astype(h.dtype))

def trunk_layer(x, cond, s0, row_w, lb, w_ada, b_ada, norm1, w_in, conv_w, conv_b,
                onorm, w_out_a, w_out_b, w_o, norm2, w_router, w_e_gate, w_e_up, w_e_down):
    D = x.shape[-1]
    mod = (jnp.dot(jax.nn.silu(cond), w_ada) + b_ada).reshape(-1, 1, 6 * D)
    sh1, sc1, g1, sh2, sc2, g2 = jnp.split(mod, 6, axis=-1)
    h = rmsnorm(x, norm1) * (1.0 + sc1) + sh1
    x_in, bg, cg, q, zf, zb, iv, og, ga, gb = split_proj(jnp.dot(h, w_in))
    ya = jnp.dot(bg * short_conv(cg * x_in, conv_w, conv_b, row_w), w_out_a)
    ob, S = hgrn2_branch(q, zf, zb, iv, og, lb, onorm, s0)
    yb = jnp.dot(ob.astype(x.dtype), w_out_b)
    mix = jnp.dot(jax.nn.sigmoid(ga) * ya + jax.nn.sigmoid(gb) * yb, w_o)
    x = x + g1 * mix
    h2 = rmsnorm(x, norm2) * (1.0 + sc2) + sh2
    x = x + g2 * expert_choice_ffn(h2, w_router, w_e_gate, w_e_up, w_e_down)
    return x, S

def setup_inputs(seed: int = 0) -> dict:
    key = jax.random.key(seed)
    ks = jax.random.split(key, 24)
    n = jax.random.normal
    D = D_MODEL
    return {
        'x_prompt': n(ks[0], (BATCH, SEQ, D), jnp.float32),
        'x_sample': n(ks[1], (DEC_BATCH, DEC_SEQ, D), jnp.float32),
        'state_hgrn': 0.5 * n(ks[2], (DEC_BATCH, DEPTH, 2, HGRN_HEADS, HGRN_DK, HGRN_DV), jnp.float32),
        'c': n(ks[3], (DEC_BATCH, D), jnp.float32),
        'c_ctx': n(ks[4], (D,), jnp.float32),
        'w_ada': 0.5 * D ** -0.5 * n(ks[5], (DEPTH, D, 6 * D), jnp.float32),
        'b_ada': 0.02 * n(ks[6], (DEPTH, 6 * D), jnp.float32),
        'norm1': 1.0 + 0.05 * n(ks[7], (DEPTH, D), jnp.float32),
        'w_in': D ** -0.5 * n(ks[8], (DEPTH, D, PROJ_TOTAL), jnp.float32),
        'conv_w': 0.5 * n(ks[9], (DEPTH, 3, CONV_WIDTH), jnp.float32),
        'conv_b': 0.02 * n(ks[10], (DEPTH, CONV_WIDTH), jnp.float32),
        'hgrn_lb': 0.1 * n(ks[11], (2, DEPTH + 1, HGRN_KW), jnp.float32),
        'hgrn_onorm': 1.0 + 0.05 * n(ks[12], (DEPTH, HGRN_VW), jnp.float32),
        'w_out_a': CONV_WIDTH ** -0.5 * n(ks[13], (DEPTH, CONV_WIDTH, D), jnp.float32),
        'w_out_b': HGRN_VW ** -0.5 * n(ks[14], (DEPTH, HGRN_VW, D), jnp.float32),
        'w_o': D ** -0.5 * n(ks[15], (DEPTH, D, D), jnp.float32),
        'norm2': 1.0 + 0.05 * n(ks[16], (DEPTH, D), jnp.float32),
        'w_router': D ** -0.5 * n(ks[17], (DEPTH, D, N_EXPERTS), jnp.float32),
        'w_e_gate': D ** -0.5 * n(ks[18], (DEPTH, N_EXPERTS, D, D_EXPERT), jnp.float32),
        'w_e_up': D ** -0.5 * n(ks[19], (DEPTH, N_EXPERTS, D, D_EXPERT), jnp.float32),
        'w_e_down': D_EXPERT ** -0.5 * n(ks[20], (DEPTH, N_EXPERTS, D_EXPERT, D), jnp.float32),
        'final_norm': 1.0 + 0.05 * n(ks[21], (D,), jnp.float32),
    }

def reference(x_prompt, x_sample, state_hgrn, c, c_ctx, w_ada, b_ada, norm1, w_in, conv_w,
              conv_b, hgrn_lb, hgrn_onorm, w_out_a, w_out_b, w_o, norm2, w_router,
              w_e_gate, w_e_up, w_e_down, final_norm):
    lb_all = jnp.cumsum(jax.nn.softmax(hgrn_lb.astype(jnp.float32), axis=1), axis=1)
    B_p, T_p, _ = x_prompt.shape
    xp = x_prompt
    xs = x_sample
    s_zero = jnp.zeros((B_p, 2, HGRN_HEADS, HGRN_DK, HGRN_DV), jnp.float32)
    ctx_states = []
    for l in range(DEPTH):
        shared = (lb_all[:, l], w_ada[l], b_ada[l], norm1[l], w_in[l], conv_w[l], conv_b[l],
                  hgrn_onorm[l], w_out_a[l], w_out_b[l], w_o[l], norm2[l], w_router[l],
                  w_e_gate[l], w_e_up[l], w_e_down[l])
        xp, S_ctx = trunk_layer(xp, c_ctx, s_zero, T_p, *shared)
        ctx_states.append(S_ctx.astype(x_prompt.dtype))
        xs, _ = trunk_layer(xs, c, state_hgrn[:, l], GRID_W, *shared)
    y_prompt = rmsnorm(xp, final_norm)
    y_sample = rmsnorm(xs, final_norm)
    new_state_hgrn = jnp.stack(ctx_states, axis=1)
    return (y_prompt, y_sample, new_state_hgrn)


_drawn_inputs = setup_inputs


def setup_inputs(seed=0):
    import zlib

    import numpy as np

    out = dict(_drawn_inputs(seed))
    spreads = {}
    factors = {'state_hgrn': 8.0, 'conv_b': 8.0, 'hgrn_onorm': 8.0, 'norm2': 5.164}
    for name, (base, spread) in spreads.items():
        noise = np.random.default_rng([zlib.crc32(name.encode()), seed]).standard_normal(out[name].shape)
        drawn = base * np.exp(spread * noise) if base else spread * noise
        out[name] = __import__('jax').numpy.asarray(drawn.astype(out[name].dtype))
    for name, factor in factors.items():
        out[name] = (out[name] * factor).astype(out[name].dtype)
    return out
```

```python
from contextlib import ExitStack

import numpy as np

import concourse.bass as bass
from concourse import mybir
from concourse.alu_op_type import AluOpType as ALU

ACT = mybir.ActivationFunctionType
AX = mybir.AxisListType
F32 = mybir.dt.float32
U32 = mybir.dt.uint32
ds = bass.ds

P = 128
D = 1024
KT = D // P
TL = 8
TN = TL + 1
CTX = TL
T = TN * P
NCH = 3
CH = T // NCH
ROW = 64
G = 4
GW = D // G
NE = 16
CAP_L = 2 * TL * P // NE
CAP_C = 2 * P // NE
EPS = 1e-6

C_ID = 0
C_ML = C_ID + P
C_ST = C_ML + 2 * 4 * P
C_MK = C_ST + 2 * P
C_ONE = C_MK + 2 * P
C_IOTA = C_ONE + 1
C_TOK = C_IOTA + P
C_END = C_TOK + TN


def shape_constants():
    c = np.zeros((P, C_END), np.float32)
    s, t = np.arange(P)[:, None], np.arange(P)[None, :]
    c[:, C_ID:C_ID + P] = s == t
    edge = (s <= t).astype(np.float32)

    def about(size, mid):
        same = s // size == t // size
        return same, ((t % size >= mid) & (s % size >= mid) & (s <= t) & same,
                      (t % size < mid) & (s % size < mid) & (s > t) & same)

    _, (after, before) = about(32, 16)
    near = after.astype(np.float32) - before
    _, (after, before) = about(128, 64)
    half = (after | before).astype(np.float32)
    _, (after, before) = about(64, 32)
    quarter = (after | before).astype(np.float32)
    fwd = [edge, near, half, quarter]
    for i, m in enumerate(fwd):
        c[:, C_ML + i * P:C_ML + (i + 1) * P] = m
        c[:, C_ML + (4 + i) * P:C_ML + (5 + i) * P] = m[::-1, ::-1]
    c[:, C_ST:C_ST + P] = s > t
    c[:, C_ST + P:C_ST + 2 * P] = s < t
    c[:, C_MK:C_MK + P] = s <= t
    c[:, C_MK + P:C_MK + 2 * P] = s >= t
    c[:, C_ONE] = 1
    c[:, C_IOTA:C_IOTA + P] = t + 1
    c[:, C_TOK:C_TOK + TN] = np.arange(P)[:, None] + P * np.arange(TN)[None, :]
    return c


class Region:

    def __init__(self, nc, start, end):
        self.nc, self.at, self.end = nc, start, end

    def __call__(self, name, shape, dtype=F32):
        size = int(np.prod(shape[1:])) * 4
        t = self.nc.alloc_sbuf_tensor_at(name, shape, dtype, offset=self.at)
        self.at += (size + 31) // 32 * 32
        assert self.at <= self.end, (name, self.at, self.end)
        return t


def trunk(nc, x_prompt, x_sample, state, cond, c_ctx, w_ada, b_ada, norm1, w_in, conv_w, conv_b,
          hgrn_lb, onorm, w_out_a, w_out_b, w_o, norm2, w_router, w_eg, w_eu, w_ed, final_norm,
          consts, y_prompt, y_sample, new_state, upto="all"):
    ctx = ExitStack()
    with ctx:
        stage_sems = []

        def lasting(name):
            return nc.alloc_semaphore(name)

        def sem(name):
            stage_sems.append(nc.alloc_semaphore(name))
            return stage_sems[-1]

        def next_stage():
            nc.clear_and_free_semaphores(list(stage_sems))
            stage_sems.clear()
            nc.all_engine_barrier()

        def scratch(name, shape):
            return nc.dram_tensor(name, shape, F32, kind="Internal").ap()

        mod_d = scratch("mod_d", [2, 4, D])
        lb_d = scratch("lb_d", [2, 2, D])
        ya_d = scratch("ya_d", [D, T])
        ob_d = scratch("ob_d", [D, T])
        x1_d = scratch("x1_d", [T, D])
        h2_d = scratch("h2_d", [T, D])

        PS = [ctx.enter_context(nc.psum_tensor(f"bank{i}", [P, 512], F32)) for i in range(8)]

        lo = (nc.sbuf_base + 63) // 64 * 64
        hi = nc.sbuf_top // 64 * 64
        keep = Region(nc, lo, hi)
        CST = keep("CST", [P, C_END])
        IDENT = CST[:, C_ID:C_ID + P]
        ONE = CST[:, C_ONE:C_ONE + 1]
        A1T = keep("A1T", [P, KT, 2])
        SH1T = keep("SH1T", [P, KT, 2])
        CW = keep("CW", [P, KT, 5])
        W_OFF = keep.at
        W = keep("W", [P, 4, KT, GW])
        HT = keep("HT", [P, KT, T])
        after_h = keep.at
        we_in = [lasting(f"we_in{i}") for i in range(12)]

        const_in = lasting("const_in")

        passed = {e: lasting(f"passed_{e}") for e in ("sp", "pool")}

        def settled(eng):
            eng.sem_inc(passed["pool" if eng is nc.gpsimd else "sp"], 1)

        weights_in = [lasting(f"weights_in{i}") for i in range(4)]

        pro = Region(nc, after_h, hi)
        AW = pro("AW", [P, 2, KT, 512])
        CR = pro("CR", [2, D])
        CE = pro("CE", [2, D])
        CT = pro("CT", [P, KT, 2])
        MODR = pro("MODR", [2, 6 * D])
        BR = pro("BR", [2, 6 * D])
        NR = pro("NR", [2, 2, D])
        LBI = pro("LBI", [16, 2, P])
        LBM = pro("LBM", [16, P])
        LBO = pro("LBO", [16, 2, P])
        LBS = pro("LBS", [16, P])
        CWR = pro("CWR", [5, D])
        XT = pro("XT", [P, 3, D])
        XJ = pro("XJ", [P, D])
        XN = pro("XN", [P, 2, D])
        XS = pro("XS", [P, TN])
        XR = pro("XR", [P, TN])
        w_ada_v = w_ada[0].rearrange("(k p) n -> p k n", p=P)
        x_rows = [x_sample[0, t * P:(t + 1) * P, :] for t in range(TL)] + [x_prompt[0]]

        rows_in = sem("rows_in")
        lbi_in = sem("lbi_in")
        ada_in = [sem(f"ada_in{i}") for i in range(2)]
        x_in_s = [sem(f"x_in{i}") for i in range(3)]
        cond_act = sem("cond_act")
        cond_silu = sem("cond_silu")
        cond_t = sem("cond_t")
        cond_ct = sem("cond_ct")
        ada_mm = sem("ada_mm")
        ada_row = sem("ada_row")
        mod_fix = sem("mod_fix")
        mod_t = sem("mod_t")
        mod_ct = sem("mod_ct")
        mod_out = sem("mod_out")
        lb_step = sem("lb_step")
        lb_exp = sem("lb_exp")
        lb_out = sem("lb_out")
        sq_done = sem("sq_done")
        rs_ln = sem("rs_ln")
        rs_done = sem("rs_done")
        xn_done = sem("xn_done")
        ht_t = sem("ht_t")
        ht_dve = sem("ht_dve")
        ht_act = sem("ht_act")

        w_in_v = w_in[0].rearrange("(k p) n -> p k n", p=P)
        XI, BG, CG, Q, ZF, ZB, IV, OG, GA, GB = (i * D for i in range(10))

        def wload(eng, slot, src, col):
            eng.dma_start(W[:, slot], src[:, :, ds(col, GW)]).then_inc(weights_in[slot], 16)

        def branch_weights(eng, g, first):
            for slot, off in enumerate((ZF, ZB, IV, Q) if first else (OG, XI, CG, BG)):
                wload(eng, slot, w_in_v, g * GW + off)

        def evac_h(eng, t, half):
            c = 0 if t == CTX else 1
            eng.wait_ge(mod_ct, 1)
            eng.wait_ge(ht_t, 2 * t + half + 1)
            for k in range(4 * half, 4 * half + 4):
                out = HT[:, k, t * P:(t + 1) * P]
                src = PS[4 + half + 2 * (t % 2)][:, (k % 4) * P:(k % 4 + 1) * P]
                if half == 0:
                    ins = nc.vector.tensor_scalar(out, src, A1T[:, k, c:c + 1],
                                                  SH1T[:, k, c:c + 1], ALU.mult, ALU.add)
                else:
                    ins = nc.scalar.activation(out, src, ACT.Identity, bias=SH1T[:, k, c:c + 1],
                                               scale=A1T[:, k, c:c + 1])
            ins.then_inc(ht_act if half else ht_dve, 1)

        with nc.Block() as block:
            @block.sync
            def _(sp):
                sp.dma_start(CST[:], consts).then_inc(const_in, 16)
                sp.dma_start(CR[0:1, :], c_ctx.rearrange("(a n) -> a n", a=1)).then_inc(rows_in, 16)
                sp.dma_start(CR[1:2, :], cond).then_inc(rows_in, 16)
                for i in range(2):
                    sp.dma_start(AW[:, i], w_ada_v[:, :, i * 512:(i + 1) * 512]).then_inc(ada_in[i], 16)
                sp.dma_start(BR[:], b_ada[0].partition_broadcast(2)).then_inc(rows_in, 16)
                sp.dma_start(NR[:, 0, :], norm1[0].partition_broadcast(2)).then_inc(rows_in, 16)
                sp.dma_start(NR[:, 1, :], norm2[0].partition_broadcast(2)).then_inc(rows_in, 16)
                for d in range(2):
                    sp.dma_start(LBI[8 * d:8 * d + 8], hgrn_lb[d].rearrange("j (c f) -> c j f", f=P)) \
                      .then_inc(lbi_in, 16)
                for t in range(3):
                    sp.dma_start(XT[:, t], x_rows[t]).then_inc(x_in_s[t], 16)
                with sp.Fori(0, 5) as j:
                    for i in range(2):
                        sp.wait_ge(ada_mm, j * 2 + i + 1)
                        sp.dma_start(AW[:, i], w_ada_v[:, :, ds(j * 1024 + (i + 2) * 512, 512)]) \
                          .then_inc(ada_in[i], 16)
                branch_weights(sp, 0, first=True)
                for t in range(3, TN):
                    sp.wait_ge(xn_done, t - 2)
                    sp.dma_start(XT[:, t % 3], x_rows[t]).then_inc(x_in_s[t % 3], 16)
                sp.wait_ge(mod_out, 64)
                sp.wait_ge(lb_out, 64)

            @block.scalar
            def _(act):
                act.preload_act_table_set("natural_log_exp_and_others")
                act.dma_start(CWR[0:3, :], conv_w[0]).then_inc(const_in, 16)
                act.dma_start(CWR[3:4, :], conv_b).then_inc(const_in, 16)
                act.dma_start(CWR[4:5, :], onorm).then_inc(const_in, 16)
                act.wait_ge(rows_in, 80)
                nc.scalar.activation(CE[:], CR[:], ACT.Exp, scale=-1.0).then_inc(cond_act, 1)
                act.wait_ge(cond_act, 1)
                nc.scalar.activation(CE[:], CE[:], ACT.Ln, bias=1.0).then_inc(cond_act, 1)
                act.wait_ge(cond_act, 2)
                nc.scalar.activation(CE[:], CE[:], ACT.Exp, scale=-1.0).then_inc(cond_act, 1)
                act.wait_ge(lb_step, 3)
                nc.scalar.activation(LBI[:], LBI[:], ACT.Exp).then_inc(lb_exp, 1)
                for t in range(TN + 1):
                    if t < TN:
                        act.wait_ge(x_in_s[t % 3], 16 * (t // 3 + 1))
                        if t:
                            act.wait_ge(sq_done, t)
                        nc.scalar.activation(XJ[:], XT[:, t % 3], ACT.Square,
                                             accum_out=XS[:, t:t + 1]).then_inc(sq_done, 1)
                        act.wait_ge(sq_done, t + 1)
                        nc.scalar.activation(XS[:, t:t + 1], XS[:, t:t + 1], ACT.Ln, bias=EPS,
                                             scale=1.0 / D).then_inc(rs_ln, 1)
                        act.wait_ge(rs_ln, t + 1)
                        nc.scalar.activation(XR[:, t:t + 1], XS[:, t:t + 1], ACT.Exp,
                                             scale=-0.5).then_inc(rs_done, 1)
                    if t > 0:
                        evac_h(act, t - 1, 1)

            @block.tensor
            def _(pe):
                pe.wait_ge(const_in, 64)
                pe.wait_ge(cond_silu, 1)
                for k in range(KT):
                    ins = nc.tensor.transpose(PS[0][:, 2 * k:2 * k + 2], CR[:, k * P:(k + 1) * P],
                                              IDENT[0:2, 0:2])
                for k in range(KT):
                    ins = nc.tensor.transpose(PS[0][:, 16 + 5 * k:21 + 5 * k], CWR[:, k * P:(k + 1) * P],
                                              IDENT[0:5, 0:5])
                ins.then_inc(cond_t, 1)
                pe.wait_ge(cond_ct, 1)
                with pe.Fori(0, 6) as j:
                    for i in range(2):
                        pe.wait_ge(ada_in[i], j * 16 + 16)
                        pe.wait_ge(ada_row, j * 2)
                        for k in range(KT):
                            ins = nc.tensor.matmul(PS[1 + i][0:2, :], CT[:, k, :], AW[:, i, k, :],
                                                   start=(k == 0), stop=(k == KT - 1))
                        ins.then_inc(ada_mm, 1)
                pe.wait_ge(mod_fix, 2)
                for k in range(KT):
                    nc.tensor.transpose(PS[3][:, 2 * k:2 * k + 2], MODR[:, k * P:(k + 1) * P],
                                        IDENT[0:2, 0:2])
                    ins = nc.tensor.transpose(PS[3][:, 16 + 2 * k:18 + 2 * k],
                                              MODR[:, D + k * P:D + (k + 1) * P], IDENT[0:2, 0:2])
                ins.then_inc(mod_t, 1)
                for t in range(TN):
                    pe.wait_ge(xn_done, t + 1)
                    for half in range(2):
                        if t >= 2:
                            pe.wait_ge(ht_act if half else ht_dve, t - 1)
                        for k in range(4 * half, 4 * half + 4):
                            ins = nc.tensor.transpose(PS[4 + half + 2 * (t % 2)][:, (k % 4) * P:(k % 4 + 1) * P],
                                                      XN[:, t % 2, k * P:(k + 1) * P], IDENT)
                        ins.then_inc(ht_t, 1)

            @block.vector
            def _(dve):
                dve.wait_ge(lbi_in, 32)
                nc.vector.tensor_tensor(LBM[:], LBI[:, 0, :], LBI[:, 1, :], ALU.max).then_inc(lb_step, 1)
                dve.wait_ge(lb_step, 1)
                for j in range(2):
                    nc.vector.tensor_tensor(LBI[:, j, :], LBI[:, j, :], LBM[:], ALU.subtract) \
                      .then_inc(lb_step, 1)
                dve.wait_ge(cond_act, 3)
                nc.vector.tensor_tensor(CR[:], CR[:], CE[:], ALU.mult).then_inc(cond_silu, 1)
                dve.wait_ge(lb_exp, 1)
                nc.vector.tensor_tensor(LBS[:], LBI[:, 0, :], LBI[:, 1, :], ALU.add).then_inc(lb_step, 1)
                dve.wait_ge(lb_step, 4)
                nc.vector.reciprocal(LBM[:], LBS[:]).then_inc(lb_step, 1)
                dve.wait_ge(lb_step, 5)
                nc.vector.tensor_tensor(LBO[:, 0, :], LBI[:, 0, :], LBM[:], ALU.mult).then_inc(lb_step, 1)
                dve.wait_ge(lb_step, 6)
                nc.vector.tensor_scalar(LBO[:, 1, :], LBO[:, 0, :], -1.0, 1.0, ALU.mult, ALU.add) \
                  .then_inc(lb_step, 1)
                dve.wait_ge(cond_t, 1)
                nc.vector.tensor_copy(CT[:].rearrange("p k c -> p (k c)"), PS[0][:, 0:2 * KT]).then_inc(cond_ct, 1)
                nc.vector.tensor_copy(CW[:].rearrange("p k c -> p (k c)"), PS[0][:, 16:16 + 5 * KT])
                with dve.Fori(0, 6) as j:
                    for i in range(2):
                        dve.wait_ge(ada_mm, j * 2 + i + 1)
                        nc.vector.tensor_tensor(MODR[:, ds(j * 1024 + i * 512, 512)], PS[1 + i][0:2, :],
                                                BR[:, ds(j * 1024 + i * 512, 512)], ALU.add).then_inc(ada_row, 1)
                dve.wait_ge(ada_row, 12)
                for j, col in enumerate((D, 4 * D)):
                    nc.vector.scalar_tensor_tensor(MODR[:, col:col + D], MODR[:, col:col + D], 1.0,
                                                   NR[:, j, :], ALU.add, ALU.mult).then_inc(mod_fix, 1)
                dve.wait_ge(mod_t, 1)
                nc.vector.tensor_copy(SH1T[:].rearrange("p k c -> p (k c)"), PS[3][:, 0:16])
                nc.vector.tensor_copy(A1T[:].rearrange("p k c -> p (k c)"), PS[3][:, 16:32]).then_inc(mod_ct, 1)
                for t in range(TN + 1):
                    if t < TN:
                        dve.wait_ge(rs_done, t + 1)
                        if t >= 2:
                            dve.wait_ge(ht_t, 2 * (t - 1))
                        nc.vector.tensor_scalar(XN[:, t % 2], XT[:, t % 3], XR[:, t:t + 1], None,
                                                ALU.mult).then_inc(xn_done, 1)
                    if t > 0:
                        evac_h(dve, t - 1, 0)

            @block.gpsimd
            def _(pool):
                pool.wait_ge(lb_step, 7)
                for d in range(2):
                    for j in range(2):
                        pool.dma_start(lb_d[j, d].rearrange("(c f) -> c f", f=P),
                                       LBO[8 * d:8 * d + 8, j, :]).then_inc(lb_out, 16)
                pool.wait_ge(mod_fix, 2)
                for i in range(4):
                    pool.dma_start(mod_d[:, i, :], MODR[:, (2 + i) * D:(3 + i) * D]).then_inc(mod_out, 16)

        next_stage()

        br = Region(nc, after_h, hi)
        QT = br("QT", [P, 2, T])
        OGT = br("OGT", [P, 2, T])
        LF = br("LF", [P, TN, 2, GW])
        KK = br("KK", [P, TN, 2, GW])
        V = br("V", [P, TN, GW])
        SS = br("SS", [P, 2, TL, 2, P])
        SC = br("SC", [P, 4, P])
        LBB = br("LBB", [P, 2, 2, GW])
        ZR = br("ZR", [P, 2, 512])
        ZG = br("ZG", [P, 2, 512])
        QR = br("QR", [P, 2, CH])
        KH = br("KH", [P, 2, 2, GW])
        DEC = br("DEC", [P, 2, 4])
        EE = br("EE", [P, 2, 5, P])
        QE = br("QE", [P, 4, 4, P])
        KE = br("KE", [P, 2, 3, P])
        SM = br("SM", [P, 4, P])
        SQJ = br("SQJ", [P, 2, P])
        SSQ = br("SSQ", [P, 2])
        RST = br("RST", [P, 2])
        ON = br("ON", [P, 2, P])
        OB = br("OB", [P, 2, 2, P])
        CWP = br("CWP", [P, 2, 5])
        CU = br("CU", [P, 2, CH])
        CC = br("CC", [P, 2, CH])
        CY = br("CY", [P, 2, CH])

        Z_STEPS = [s for t in range(TN) for s in (("z", t), ("v", t))]
        QO_STEPS = [("q", m, n) for m in range(2) for n in range(NCH)] + \
                   [("o", m, n) for m in range(2) for n in range(NCH)]
        A_STEPS = [(k, m, n) for m in range(2) for n in range(NCH) for k in ("x", "c", "b")]
        STEPS = Z_STEPS + QO_STEPS + A_STEPS
        NS = len(STEPS)
        assert NS % 2 == 0
        P1 = list(range(TL - 1)) + [CTX]
        N1 = len(P1)

        pair_done = {e: sem(f"pair_done_{e}") for e in ("pe", "act", "dve", "pool")}
        product = sem("product")
        z_read = sem("z_read")
        z_ln = sem("z_ln")
        z_sig = sem("z_sig")
        z_gate = sem("z_gate")
        k_made = sem("k_made")
        f_made = sem("f_made")
        lf_made = sem("lf_made")
        v_read = sem("v_read")
        qo_exp = sem("qo_exp")
        qo_ln = sem("qo_ln")
        qo_sig = sem("qo_sig")
        qo_read = sem("qo_read")
        x_read = sem("x_read")
        cg_read = sem("cg_read")
        tap1 = sem("tap1")
        conv_done = sem("conv_done")
        bg_read = sem("bg_read")
        tail_sum = sem("tail_sum")
        tail_read = sem("tail_read")
        khat = sem("khat")
        ds_done = sem("ds_done")
        state_upd = sem("state_upd")
        k_t = sem("k_t")
        e_sum = sem("e_sum")
        e_exp = sem("e_exp")
        qk_dec = sem("qk_dec")
        scores = sem("scores")
        masked = sem("masked")
        o_done = sem("o_done")
        o_sq = sem("o_sq")
        o_ln = sem("o_ln")
        o_rs = sem("o_rs")
        o_norm = sem("o_norm")
        o_t = sem("o_t")
        ob_made = sem("ob_made")
        cols_made = sem("cols_made")
        lb_in = sem("lb_in")
        st_in = sem("st_in")
        ya_out = [sem(f"ya_out{i}") for i in range(2)]
        ob_out = [sem(f"ob_out{i}") for i in range(2)]
        sc_out = sem("sc_out")

        def tile_of(s, d):
            return s if s == CTX or d == 0 else TL - 1 - s

        w_oa_v, w_ob_v, w_o_v = (w[0].rearrange("(k p) n -> p k n", p=P) for w in (w_out_a, w_out_b, w_o))

        def merge_weights(eng, slot, g):
            src, off = ((w_in_v, GA), (w_oa_v, 0), (w_in_v, GB), (w_ob_v, 0))[slot]
            wload(eng, slot, src, g * GW + off)

        w_e_v = [w[0].rearrange("e (k p) n -> p e k n", p=P) for w in (w_ed, w_eg, w_eu)]

        def expert_weights(eng, slot, e):
            eng.dma_start(WE[:, slot], w_e_v[slot // 4][:, ds(e, 1), :, (slot % 4) * GW:(slot % 4 + 1) * GW]
                          .rearrange("p e k n -> p (e k) n")).then_inc(we_in[slot], 16)

        def ob_store(eng, g, t):
            eng.wait_ge(ob_made, g * TN + t + 1)
            eng.dma_start(ob_d[ds(g * GW, GW), t * P:(t + 1) * P].rearrange("(a p) n -> p a n", p=P),
                          OB[:, t % 2]).then_inc(ob_out[t % 2], 16)

        conv_left = sem("conv_left")

        def step_no(step):
            return STEPS.index(step)

        def release(eng, g, j):
            kind = STEPS[j][0]
            before = sum(1 for s in STEPS[:j + 1] if s[0] == kind)
            if kind in "qo":
                before = sum(1 for s in STEPS[:j + 1] if s[0] in "qo")
            s, per = {"z": (z_read, TN), "v": (v_read, TN), "q": (qo_read, 12), "o": (qo_read, 12),
                      "x": (x_read, 6), "c": (cg_read, 6), "b": (bg_read, 6)}[kind]
            eng.wait_ge(s, g * per + before)

        with nc.Block() as block:
            @block.sync
            def _(sp):
                def pair(g, last):
                    for e in ("pe", "dve", "pool"):
                        sp.wait_ge(pair_done[e], g)
                    for j in range(2):
                        for d in range(2):
                            sp.dma_start(LBB[:, j, d, :],
                                         lb_d[j, d, ds(g * GW, GW)].partition_broadcast(P)).then_inc(lb_in, 16)
                    for d in range(2):
                        sp.dma_start(SS[:, d, 0 if d == 0 else TL - 1],
                                     state[0, 0, d, ds(2 * g, 2)].rearrange("a k v -> k a v")).then_inc(st_in, 16)
                    for slot, (last_use, off) in enumerate(
                            ((("z", TN - 1), OG), (("z", TN - 1), XI), (("v", TN - 1), CG),
                             (("q", 1, NCH - 1), BG))):
                        sp.wait_ge(product, g * NS + step_no(last_use) + 1)
                        wload(sp, slot, w_in_v, g * GW + off)
                    sp.wait_ge(state_upd, g * N1 + N1)
                    for d in range(2):
                        sp.dma_start(new_state[0, 0, d, ds(2 * g, 2)].rearrange("a k v -> k a v"),
                                     SC[:, 2 * d:2 * d + 2]).then_inc(sc_out, 16)
                    def reload(slot, step):
                        sp.wait_ge(product, g * NS + step_no(step) + 1)
                        if last:
                            merge_weights(sp, slot, 0)
                        else:
                            wload(sp, slot, w_in_v, (g + 1) * GW + (ZF, ZB, IV, Q)[slot])

                    reload(0, ("o", 1, NCH - 1))
                    i = 0
                    for t in range(TN):
                        for step in A_STEPS[2 * t:2 * t + 2]:
                            kind, m, n = step
                            if kind == "b":
                                sp.wait_ge(bg_read, g * 6 + i + 1)
                                sp.dma_start(ya_d[ds(g * GW + m * P, P), n * CH:(n + 1) * CH], CY[:, i % 2]) \
                                  .then_inc(ya_out[i % 2], 16)
                                i += 1
                            if (m, n) == (1, NCH - 1):
                                reload({"x": 1, "c": 2, "b": 3}[kind], step)
                        if t:
                            ob_store(sp, g, t - 1)
                    ob_store(sp, g, TN - 1)

                with sp.Fori(0, G - 1) as g:
                    pair(g, False)
                pair(G - 1, True)
                sp.wait_ge(sc_out, 32 * G)
                for i in range(2):
                    sp.wait_ge(ya_out[i], G * 48)
                    sp.wait_ge(ob_out[i], G * 16 * (5 - i))

            @block.tensor
            def _(pe):
                def product_step(g, j):
                    kind, *at = STEPS[j]
                    if j >= 2:
                        release(pe, g, j - 2)
                    bank = PS[j % 2]
                    if kind in "zv":
                        t, = at
                        if t == 0:
                            for slot in ((0, 1) if kind == "z" else (2,)):
                                pe.wait_ge(weights_in[slot], g * 32 + 16)
                        for k in range(KT):
                            rhs, out = (W[:, 0:2, k, :], bank[:]) if kind == "z" else (W[:, 2, k, :], bank[:, 0:GW])
                            ins = nc.tensor.matmul(out, HT[:, k, t * P:(t + 1) * P], rhs,
                                                   start=(k == 0), stop=(k == KT - 1))
                    else:
                        m, n = at
                        slot = {"q": 3, "o": 0, "x": 1, "c": 2, "b": 3}[kind]
                        if m == 0 and n == 0:
                            pe.wait_ge(weights_in[slot], g * 32 + (16 if kind == "q" else 32))
                        for k in range(KT):
                            ins = nc.tensor.matmul(bank[:, 0:CH], W[:, slot, k, m * P:(m + 1) * P],
                                                   HT[:, k, n * CH:(n + 1) * CH],
                                                   start=(k == 0), stop=(k == KT - 1))
                    ins.then_inc(product, 1)

                def tails(g, i):
                    s = P1[i]
                    if i == 0:
                        pe.wait_ge(lf_made, g * TN + TN)
                    if i >= 2:
                        pe.wait_ge(tail_read, g * N1 + i - 1)
                    elif i == 1:
                        pe.wait_ge(tail_read, g * N1 + i)
                    for d in range(2):
                        t = tile_of(s, d)
                        nc.tensor.matmul(PS[2 + i % 2][:, d * GW:(d + 1) * GW],
                                         CST[:, C_ST + d * P:C_ST + (d + 1) * P], LF[:, t, d, :],
                                         start=True, stop=True)
                    if i >= 1:
                        pe.wait_ge(tail_read, g * N1 + i)
                    for d in range(2):
                        t = tile_of(s, d)
                        for a in range(2):
                            ins = nc.tensor.matmul(PS[4][:, 2 * d + a:2 * d + a + 1],
                                                   LF[:, t, d, a * P:(a + 1) * P], ONE, start=True, stop=True)
                    ins.then_inc(tail_sum, 1)

                def contribution(g, i):
                    s = P1[i]
                    pe.wait_ge(khat, g * N1 + i + 1)
                    if i >= 2:
                        pe.wait_ge(state_upd, g * N1 + i - 1)
                    for d in range(2):
                        t = tile_of(s, d)
                        for a in range(2):
                            da = 2 * d + a
                            ins = nc.tensor.matmul(PS[5 + i % 2][:, da * P:(da + 1) * P],
                                                   KH[:, i % 2, d, a * P:(a + 1) * P], V[:, t, a * P:(a + 1) * P],
                                                   start=True, stop=True)
                    ins.then_inc(ds_done, 1)

                def exponents(g, t, da):
                    d, a = da // 2, da % 2
                    if t or da >= 2:
                        pe.wait_ge(e_exp, g * 4 * TN + 4 * t + da - 1)
                    nc.tensor.matmul(PS[2 + da % 2][:], LF[:, t, d, a * P:(a + 1) * P],
                                     CST[:, C_ML + d * 512:C_ML + (d + 1) * 512],
                                     start=True, stop=True).then_inc(e_sum, 1)

                def keys_t(g, t):
                    if t:
                        pe.wait_ge(qk_dec, g * 4 * TN + 4 * t)
                    for da in range(4):
                        ins = nc.tensor.transpose(PS[4][:, da * P:(da + 1) * P],
                                                  KK[:, t, da // 2, (da % 2) * P:(da % 2 + 1) * P], IDENT)
                    ins.then_inc(k_t, 1)

                def score(g, t, da):
                    pe.wait_ge(qk_dec, g * 4 * TN + 4 * t + da + 1)
                    if da == 0 and t:
                        pe.wait_ge(masked, g * TN + t)
                    q, k, out = QE[:, da], KE[:, da % 2], PS[5][:, da * P:(da + 1) * P]
                    nc.tensor.matmul(out, k[:, 0, :], q[:, 2, :], start=True, stop=True)
                    for j in range(2):
                        b = slice(64 * j, 64 * j + 64)
                        nc.tensor.matmul(out[b, b], k[:, 1, b], q[:, 3, b], start=True, stop=True)
                    for j in range(4):
                        b = slice(32 * j, 32 * j + 32)
                        ins = nc.tensor.matmul(out[b, b], k[:, 2, b], q[:, 1, b], start=True, stop=True)
                    ins.then_inc(scores, 1)

                def outputs(g, t):
                    pe.wait_ge(masked, g * TN + t + 1)
                    if t:
                        pe.wait_ge(o_norm, g * TN + t)
                    for a in range(2):
                        parts = []
                        for d in range(2):
                            if t != CTX:
                                parts.append((QE[:, 2 * d + a, 0, :], SS[:, d, t, a, :]))
                            parts.append((SM[:, 2 * d + a, :], V[:, t, a * P:(a + 1) * P]))
                        for i, (l, r) in enumerate(parts):
                            ins = nc.tensor.matmul(PS[6][:, a * P:(a + 1) * P], l, r, start=(i == 0),
                                                   stop=(i == len(parts) - 1))
                    ins.then_inc(o_done, 1)

                def outputs_t(g, t):
                    pe.wait_ge(o_norm, g * TN + t + 1)
                    if t:
                        pe.wait_ge(ob_made, g * TN + t)
                    for a in range(2):
                        ins = nc.tensor.transpose(PS[7][:, a * P:(a + 1) * P], ON[:, a, :], IDENT)
                    ins.then_inc(o_t, 1)

                with pe.Fori(0, G) as g:
                    for e in ("act", "dve", "pool"):
                        pe.wait_ge(pair_done[e], g)
                    fill = iter(range(NS))
                    for _ in Z_STEPS:
                        product_step(g, next(fill))
                    for i in range(N1):
                        tails(g, i)
                        product_step(g, next(fill))
                        if i < len(QO_STEPS) - N1:
                            product_step(g, next(fill))
                        contribution(g, i)
                    for t in range(TN):
                        keys_t(g, t)
                        exponents(g, t, 0)
                        exponents(g, t, 1)
                        if t:
                            outputs(g, t - 1)
                        product_step(g, next(fill))
                        score(g, t, 0)
                        exponents(g, t, 2)
                        score(g, t, 1)
                        exponents(g, t, 3)
                        if t:
                            outputs_t(g, t - 1)
                        product_step(g, next(fill))
                        score(g, t, 2)
                        score(g, t, 3)
                    outputs(g, TN - 1)
                    outputs_t(g, TN - 1)
                    pe.wait_ge(o_t, g * TN + TN)
                    pe.sem_inc(pair_done["pe"], 1)

            @block.scalar
            def _(act):
                def sigmoid_z(g, t):
                    b = ZR[:, t % 2]
                    act.wait_ge(product, g * NS + step_no(("z", t)) + 1)
                    if t >= 2:
                        act.wait_ge(z_gate, g * TN + t - 1)
                    nc.scalar.activation(b, PS[step_no(("z", t)) % 2][:], ACT.Exp, scale=-1.0).then_inc(z_read, 1)
                    act.wait_ge(z_read, g * TN + t + 1)
                    nc.scalar.activation(b, b, ACT.Ln, bias=1.0).then_inc(z_ln, 1)
                    if t:
                        log_f(g, t - 1)
                    act.wait_ge(z_ln, g * TN + t + 1)
                    nc.scalar.activation(b, b, ACT.Exp, scale=-1.0).then_inc(z_sig, 1)

                def log_f(g, t):
                    act.wait_ge(f_made, g * TN + t + 1)
                    nc.scalar.activation(LF[:, t].rearrange("p d n -> p (d n)"), ZG[:, t % 2], ACT.Ln) \
                      .then_inc(lf_made, 1)

                def sigmoid_qo(g, i):
                    j = len(Z_STEPS) + i
                    b = QR[:, i % 2]
                    act.wait_ge(product, g * NS + j + 1)
                    if i >= 2:
                        act.wait_ge(qo_read, g * 12 + i - 1)
                    nc.scalar.activation(b, PS[j % 2][:, 0:CH], ACT.Exp, scale=-1.0).then_inc(qo_exp, 1)
                    act.wait_ge(qo_exp, g * 12 + i + 1)
                    nc.scalar.activation(b, b, ACT.Ln, bias=1.0).then_inc(qo_ln, 1)
                    act.wait_ge(qo_ln, g * 12 + i + 1)
                    nc.scalar.activation(b, b, ACT.Exp, scale=-1.0).then_inc(qo_sig, 1)

                def tail_exp(g, i):
                    act.wait_ge(tail_sum, g * N1 + i + 1)
                    if i >= 2:
                        act.wait_ge(ds_done, g * N1 + i - 1)
                        act.wait_ge(state_upd, g * N1 + i - 1)
                    nc.scalar.activation(KH[:, i % 2].rearrange("p d n -> p (d n)"), PS[2 + i % 2][:], ACT.Exp)
                    nc.scalar.activation(DEC[:, i % 2], PS[4][:, 0:4], ACT.Exp).then_inc(tail_read, 1)

                def level_exp(g, t, da):
                    e = EE[:, da % 2]
                    n = g * 4 * TN + 4 * t + da
                    act.wait_ge(e_sum, n + 1)
                    if t or da >= 2:
                        act.wait_ge(qk_dec, n - 1)
                    nc.scalar.activation(e[:, 0:4, :], PS[2 + da % 2][:], ACT.Exp)
                    nc.scalar.activation(e[:, 4, :], PS[2 + da % 2][:, P:2 * P], ACT.Exp,
                                         scale=-1.0).then_inc(e_exp, 1)

                def conv_act(g, j):
                    kind, m, n = STEPS[j]
                    i = m * NCH + n
                    if kind == "x":
                        act.wait_ge(product, g * NS + j + 1)
                        if i >= 2:
                            act.wait_ge(conv_done, g * 6 + i - 1)
                        nc.scalar.activation(CU[:, i % 2], PS[j % 2][:, 0:CH], ACT.Copy).then_inc(x_read, 1)
                    elif kind == "c":
                        act.wait_ge(cols_made, g + 1)
                        act.wait_ge(cg_read, g * 6 + i + 1)
                        if i >= 2:
                            act.wait_ge(bg_read, g * 6 + i - 1)
                        nc.scalar.activation(CC[:, i % 2], CU[:, i % 2], ACT.Identity,
                                             bias=CWP[:, m, 3:4],
                                             scale=CWP[:, m, 1:2]).then_inc(tap1, 1)

                def o_rstd(g, t):
                    act.wait_ge(o_done, g * TN + t + 1)
                    if t:
                        act.wait_ge(o_rs, g * TN + t)
                    for a in range(2):
                        ins = nc.scalar.activation(SQJ[:, a], PS[6][:, a * P:(a + 1) * P], ACT.Square,
                                                   accum_out=SSQ[:, a:a + 1])
                    ins.then_inc(o_sq, 1)
                    act.wait_ge(o_sq, g * TN + t + 1)
                    nc.scalar.activation(SSQ[:], SSQ[:], ACT.Ln, bias=EPS, scale=1.0 / P).then_inc(o_ln, 1)
                    act.wait_ge(o_ln, g * TN + t + 1)
                    if t:
                        act.wait_ge(o_norm, g * TN + t)
                    nc.scalar.activation(RST[:], SSQ[:], ACT.Exp, scale=-0.5).then_inc(o_rs, 1)

                with act.Fori(0, G) as g:
                    for e in ("pe", "dve", "pool"):
                        act.wait_ge(pair_done[e], g)
                    for t in range(TN):
                        sigmoid_z(g, t)
                    log_f(g, TN - 1)
                    i = 0
                    for s in range(N1):
                        tail_exp(g, s)
                        for _ in range(2 if s < len(QO_STEPS) - N1 else 1):
                            sigmoid_qo(g, i)
                            i += 1
                    j = len(Z_STEPS) + len(QO_STEPS)
                    for t in range(TN):
                        level_exp(g, t, 0)
                        level_exp(g, t, 1)
                        if t:
                            o_rstd(g, t - 1)
                        conv_act(g, j)
                        level_exp(g, t, 2)
                        level_exp(g, t, 3)
                        conv_act(g, j + 1)
                        j += 2
                    o_rstd(g, TN - 1)
                    act.wait_ge(o_rs, g * TN + TN)
                    act.sem_inc(pair_done["act"], 1)

            @block.vector
            def _(dve):
                def gate_z(g, t):
                    omlb = LBB[:, 1].rearrange("p d n -> p (d n)")
                    if t == 0:
                        dve.wait_ge(lb_in, g * 64 + 64)
                    dve.wait_ge(z_sig, g * TN + t + 1)
                    if t >= 2:
                        dve.wait_ge(lf_made, g * TN + t - 1)
                        dve.wait_ge(k_made, g * TN + t - 1)
                    nc.vector.tensor_tensor(ZG[:, t % 2], ZR[:, t % 2], omlb, ALU.mult).then_inc(z_gate, 1)
                    dve.wait_ge(z_gate, g * TN + t + 1)
                    nc.vector.tensor_tensor(KK[:, t].rearrange("p d n -> p (d n)"), omlb, ZG[:, t % 2],
                                            ALU.subtract).then_inc(k_made, 1)

                def copy_v(g, t):
                    dve.wait_ge(product, g * NS + step_no(("v", t)) + 1)
                    nc.vector.tensor_copy(V[:, t], PS[step_no(("v", t)) % 2][:, 0:GW]).then_inc(v_read, 1)

                def silu_qo(g, i):
                    j = len(Z_STEPS) + i
                    kind, m, n = STEPS[j]
                    src = PS[j % 2][:, 0:CH]
                    dve.wait_ge(qo_sig, g * 12 + i + 1)
                    if kind == "q":
                        ins = nc.vector.tensor_tensor(QT[:, m, n * CH:(n + 1) * CH], src, QR[:, i % 2], ALU.mult)
                    else:
                        ins = nc.vector.scalar_tensor_tensor(OGT[:, m, n * CH:(n + 1) * CH], src,
                                                             CWP[:, m, 4:5], QR[:, i % 2],
                                                             ALU.mult, ALU.mult)
                    ins.then_inc(qo_read, 1)

                def update(g, i):
                    s = P1[i]
                    dve.wait_ge(ds_done, g * N1 + i + 1)
                    if i == 0:
                        dve.wait_ge(st_in, g * 32 + 32)
                    else:
                        dve.wait_ge(state_upd, g * N1 + i)
                    src = PS[5 + i % 2]
                    if s == CTX:
                        dve.wait_ge(sc_out, g * 32)
                        nc.vector.tensor_copy(SC[:].rearrange("p d v -> p (d v)"), src[:]).then_inc(state_upd, 1)
                        return
                    for d in range(2):
                        here = tile_of(s, d)
                        there = here + (1 if d == 0 else -1)
                        for a in range(2):
                            da = 2 * d + a
                            ins = nc.vector.scalar_tensor_tensor(
                                SS[:, d, there, a, :], SS[:, d, here, a, :], DEC[:, i % 2, da:da + 1],
                                src[:, da * P:(da + 1) * P], ALU.mult, ALU.add)
                    ins.then_inc(state_upd, 1)

                def decayed(g, t, da):
                    d, a = da // 2, da % 2
                    n = g * 4 * TN + 4 * t + da
                    e = EE[:, da % 2]
                    dve.wait_ge(e_exp, n + 1)
                    if da == 0:
                        dve.wait_ge(k_t, g * TN + t + 1)
                    if da == 0 and t:
                        dve.wait_ge(o_done, g * TN + t)
                    if t or da >= 2:
                        dve.wait_ge(scores, n - 1)
                    q = QT[:, a, t * P:(t + 1) * P].unsqueeze(1).to_broadcast([P, 4, P])
                    nc.vector.tensor_tensor(QE[:, da], q, e[:, 0:4, :], ALU.mult)
                    k = PS[4][:, da * P:(da + 1) * P].unsqueeze(1).to_broadcast([P, 3, P])
                    nc.vector.tensor_tensor(KE[:, da % 2], k, e[:, 2:5, :], ALU.mult).then_inc(qk_dec, 1)

                def mask(g, t):
                    dve.wait_ge(scores, g * 4 * TN + 4 * t + 4)
                    if t:
                        dve.wait_ge(o_done, g * TN + t)
                    m = CST[:, C_MK:C_MK + 2 * P].rearrange("p (d n) -> p d n", d=2) \
                        .unsqueeze(2).to_broadcast([P, 2, 2, P])
                    nc.vector.tensor_tensor(SM[:].rearrange("p (d a) n -> p d a n", d=2),
                                            PS[5][:].rearrange("p (d a n) -> p d a n", d=2, a=2), m,
                                            ALU.mult).then_inc(masked, 1)

                def normed(g, t):
                    dve.wait_ge(o_rs, g * TN + t + 1)
                    if t:
                        dve.wait_ge(o_t, g * TN + t)
                    for a in range(2):
                        ins = nc.vector.tensor_scalar(ON[:, a], PS[6][:, a * P:(a + 1) * P], RST[:, a:a + 1],
                                                      None, ALU.mult)
                    ins.then_inc(o_norm, 1)

                def gated(g, t):
                    dve.wait_ge(o_t, g * TN + t + 1)
                    if t >= 2:
                        dve.wait_ge(ob_out[t % 2], g * 16 * (5 - t % 2) + 16 * (t // 2))
                    else:
                        dve.wait_ge(ob_out[t % 2], g * 16 * (5 - t % 2))
                    nc.vector.tensor_tensor(OB[:, t % 2], PS[7][:, 0:2 * P].rearrange("p (a n) -> p a n", a=2),
                                            OGT[:, :, t * P:(t + 1) * P], ALU.mult).then_inc(ob_made, 1)

                def conv_dve(g, j):
                    kind, m, n = STEPS[j]
                    i = m * NCH + n
                    u, c, y = CU[:, i % 2], CC[:, i % 2], CY[:, i % 2]
                    tap = [CWP[:, m, k:k + 1] for k in range(3)]
                    if kind == "c":
                        dve.wait_ge(product, g * NS + j + 1)
                        dve.wait_ge(x_read, g * 6 + i + 1)
                        nc.vector.tensor_tensor(u, u, PS[j % 2][:, 0:CH], ALU.mult).then_inc(cg_read, 1)
                    if kind == "b":
                        cuts = [(0, CH, ROW)] if n < NCH - 1 else [(0, CH - P, ROW), (CH - P, CH, P)]
                        dve.wait_ge(tap1, g * 6 + i + 1)
                        for lo_, hi_, row in cuts:
                            cv = c[:, lo_:hi_].rearrange("p (r w) -> p r w", w=row)
                            uv = u[:, lo_:hi_].rearrange("p (r w) -> p r w", w=row)
                            ins = nc.vector.scalar_tensor_tensor(cv[:, :, 1:], uv[:, :, :row - 1], tap[0],
                                                                 cv[:, :, 1:], ALU.mult, ALU.add)
                        ins.then_inc(conv_left, 1)
                        dve.wait_ge(conv_left, g * 6 + i + 1)
                        for lo_, hi_, row in cuts:
                            cv = c[:, lo_:hi_].rearrange("p (r w) -> p r w", w=row)
                            uv = u[:, lo_:hi_].rearrange("p (r w) -> p r w", w=row)
                            ins = nc.vector.scalar_tensor_tensor(cv[:, :, :row - 1], uv[:, :, 1:], tap[2],
                                                                 cv[:, :, :row - 1], ALU.mult, ALU.add)
                        ins.then_inc(conv_done, 1)
                        dve.wait_ge(conv_done, g * 6 + i + 1)
                        dve.wait_ge(product, g * NS + j + 1)
                        if i >= 2:
                            dve.wait_ge(ya_out[i % 2], g * 48 + 16 * (i // 2))
                        else:
                            dve.wait_ge(ya_out[i % 2], g * 48)
                        nc.vector.tensor_tensor(y, c, PS[j % 2][:, 0:CH], ALU.mult).then_inc(bg_read, 1)

                with dve.Fori(0, G) as g:
                    for e in ("pe", "act", "pool"):
                        dve.wait_ge(pair_done[e], g)
                    nc.vector.tensor_scalar(CWP[:], CW[:, ds(2 * g, 2), :], 1.0, None, ALU.mult) \
                      .then_inc(cols_made, 1)
                    dve.wait_ge(cols_made, g + 1)
                    for t in range(TN):
                        gate_z(g, t)
                        copy_v(g, t)
                    i = 0
                    for s in range(N1):
                        for _ in range(2 if s < len(QO_STEPS) - N1 else 1):
                            silu_qo(g, i)
                            i += 1
                        update(g, s)
                    j = len(Z_STEPS) + len(QO_STEPS)
                    for t in range(TN):
                        decayed(g, t, 0)
                        decayed(g, t, 1)
                        if t:
                            normed(g, t - 1)
                        conv_dve(g, j)
                        decayed(g, t, 2)
                        decayed(g, t, 3)
                        if t:
                            gated(g, t - 1)
                        conv_dve(g, j + 1)
                        j += 2
                        mask(g, t)
                    normed(g, TN - 1)
                    gated(g, TN - 1)
                    dve.wait_ge(ob_made, g * TN + TN)
                    dve.sem_inc(pair_done["dve"], 1)

            @block.gpsimd
            def _(pool):
                def forget(g, t):
                    if t == 0:
                        pool.wait_ge(lb_in, g * 64 + 64)
                    pool.wait_ge(k_made, g * TN + t + 1)
                    nc.gpsimd.tensor_tensor(ZG[:, t % 2], ZG[:, t % 2], LBB[:, 0].rearrange("p d n -> p (d n)"),
                                            ALU.add).then_inc(f_made, 1)

                def key_hat(g, i):
                    s = P1[i]
                    pool.wait_ge(tail_read, g * N1 + i + 1)
                    for d in range(2):
                        ins = nc.gpsimd.tensor_tensor(KH[:, i % 2, d], KH[:, i % 2, d],
                                                      KK[:, tile_of(s, d), d, :], ALU.mult)
                    ins.then_inc(khat, 1)

                with pool.Fori(0, G) as g:
                    for e in ("pe", "act", "dve"):
                        pool.wait_ge(pair_done[e], g)
                    for t in range(TN):
                        forget(g, t)
                    for i in range(N1):
                        key_hat(g, i)
                    pool.wait_ge(khat, g * N1 + N1)
                    pool.sem_inc(pair_done["pool"], 1)

        if upto == "branches":
            return

        next_stage()

        MIX = nc.alloc_sbuf_tensor_at("MIX", [P, KT, T], F32, offset=hi - KT * T * 4)
        mg = Region(nc, after_h, hi - KT * T * 4)
        YA = mg("YA", [P, KT, T])
        OBT = mg("OBT", [P, KT, T])
        GT = mg("GT", [P, 2, 2, CH])
        MP = mg("MP", [P, 2, 2, CH])
        M_STEPS = [(kind, m, n) for m in range(2) for n in range(NCH) for kind in range(4)]
        MS = len(M_STEPS)
        W_BASE = 16 * 2 * G
        ya_in = sem("ya_in")
        ob_in = sem("ob_in")
        m_product = sem("m_product")
        m_exp = sem("m_exp")
        m_ln = sem("m_ln")
        m_sig = sem("m_sig")
        m_part = sem("m_part")
        m_sum = sem("m_sum")

        with nc.Block() as block:
            @block.sync
            def _(sp):
                for k in range(KT):
                    sp.dma_start(YA[:, k, :], ya_d[k * P:(k + 1) * P, :]).then_inc(ya_in, 16)
                    sp.dma_start(OBT[:, k, :], ob_d[k * P:(k + 1) * P, :]).then_inc(ob_in, 16)
                with sp.Fori(0, G - 1) as g:
                    for slot in range(4):
                        sp.wait_ge(m_product, g * MS + MS - 3 + slot)
                        settled(sp)
                        merge_weights(sp, slot, g + 1)
                for slot in range(4):
                    sp.wait_ge(m_product, G * MS - 3 + slot)
                    wload(sp, slot, w_o_v, slot * GW)

            @block.tensor
            def _(pe):
                with pe.Fori(0, G) as g:
                    for j, (kind, m, n) in enumerate(M_STEPS):
                        i = j // 4
                        if j < 4:
                            pe.wait_ge(weights_in[kind], W_BASE + 16 + g * 16)
                            if kind == 1:
                                pe.wait_ge(ya_in, 16 * KT)
                            if kind == 3:
                                pe.wait_ge(ob_in, 16 * KT)
                        if i >= 2:
                            if kind % 2 == 0:
                                pe.wait_ge(m_exp, g * 12 + 2 * (i - 2) + kind // 2 + 1)
                            else:
                                pe.wait_ge(m_part, g * 12 + 2 * (i - 2) + kind // 2 + 1)
                        else:
                            pe.wait_ge(m_exp if kind % 2 == 0 else m_part, g * 12)
                        src = (HT, YA, HT, OBT)[kind]
                        for k in range(KT):
                            ins = nc.tensor.matmul(PS[kind + 4 * (i % 2)][:, 0:CH], W[:, kind, k, m * P:(m + 1) * P],
                                                   src[:, k, n * CH:(n + 1) * CH], start=(k == 0),
                                                   stop=(k == KT - 1))
                        ins.then_inc(m_product, 1)

            @block.scalar
            def _(act):
                with act.Fori(0, G) as g:
                    for i in range(6):
                        for h in range(2):
                            n = g * 12 + 2 * i + h
                            b = GT[:, h, i % 2]
                            act.wait_ge(m_product, g * MS + 4 * i + 2 * h + 1)
                            act.wait_ge(m_part, g * 12 + (max(2 * (i - 2) + h + 1, 0) if i >= 2 else 0))
                            nc.scalar.activation(b, PS[2 * h + 4 * (i % 2)][:, 0:CH], ACT.Exp,
                                                 scale=-1.0).then_inc(m_exp, 1)
                            act.wait_ge(m_exp, n + 1)
                            nc.scalar.activation(b, b, ACT.Ln, bias=1.0).then_inc(m_ln, 1)
                            act.wait_ge(m_ln, n + 1)
                            nc.scalar.activation(b, b, ACT.Exp, scale=-1.0).then_inc(m_sig, 1)

            @block.vector
            def _(dve):
                with dve.Fori(0, G) as g:
                    for i, (m, n) in enumerate((m, n) for m in range(2) for n in range(NCH)):
                        for h in range(2):
                            c = g * 12 + 2 * i + h + 1
                            dve.wait_ge(m_product, g * MS + 4 * i + 2 * h + 2)
                            dve.wait_ge(m_sig, c)
                            nc.vector.tensor_tensor(MP[:, h, i % 2], PS[2 * h + 1 + 4 * (i % 2)][:, 0:CH],
                                                    GT[:, h, i % 2], ALU.mult).then_inc(m_part, 1)
                        dve.wait_ge(m_part, g * 12 + 2 * i + 2)
                        nc.vector.tensor_tensor(MIX[:, ds(2 * g + m, 1), n * CH:(n + 1) * CH],
                                                MP[:, 0, i % 2].unsqueeze(1), MP[:, 1, i % 2].unsqueeze(1),
                                                ALU.add).then_inc(m_sum, 1)

        next_stage()

        WE = nc.alloc_sbuf_tensor_at("WE", [P, 12, KT, GW], F32, offset=W_OFF)
        mx = Region(nc, W_OFF + 12 * KT * GW * 4, hi - KT * T * 4)
        TA = mx("TA", [P, TN, NE + 1, 2])
        POST = mx("POST", [P, TN, NE + 1])
        after_ta = mx.at
        G1 = mx("G1", [P, 2, D])
        SH2 = mx("SH2", [P, 2, D])
        A2 = mx("A2", [P, 2, D])
        XL = mx("XL", [P, 2, D])
        X1 = mx("X1", [P, 2, D])
        H2 = mx("H2", [P, 2, D])
        XJ2 = mx("XJ2", [P, D])
        H2T = mx("H2T", [P, KT, P])
        WR = mx("WR", [P, KT, NE])
        RS2 = mx("RS2", [P, 2, TN])
        SMX = mx("SMX", [P, 3, TN])
        LEX = mx("LEX", [P, 2, NE])
        AFT = mx("AFT", [NE, T])
        sl = Region(nc, hi - KT * T * 4, hi)
        WK = sl("WK", [NE, T])
        SEL = sl("SEL", [NE, T])
        CUM = sl("CUM", [NE, T])
        M8 = sl("M8", [NE, 2, 8])

        modv_in = sem("modv_in")
        wr_in = sem("wr_in")
        xl_in = [sem(f"xl_in{i}") for i in range(2)]
        mix_mm = sem("mix_mm")
        x1_g = sem("x1_g")
        x1_made = sem("x1_made")
        x1_out = [sem(f"x1_out{i}") for i in range(2)]
        n2_sq = sem("n2_sq")
        n2_ln = sem("n2_ln")
        n2_rs = sem("n2_rs")
        h2_a = sem("h2_a")
        h2_made = sem("h2_made")
        h2_out = [sem(f"h2_out{i}") for i in range(2)]
        h2_t = sem("h2_t")
        h2_sb = sem("h2_sb")
        logits = sem("logits")
        lg_max = sem("lg_max")
        lg_exp = sem("lg_exp")
        lg_rec = sem("lg_rec")
        aff_made = sem("aff_made")
        aff_t = sem("aff_t")
        aft_made = sem("aft_made")
        topk = sem("topk")
        ta_init = sem("ta_init")
        pos_made = sem("pos_made")
        pos_t = sem("pos_t")
        post_made = sem("post_made")
        ORDER = [CTX] + list(range(TL))

        with nc.Block() as block:
            @block.sync
            def _(sp):
                for i, dst in enumerate((G1, SH2, A2)):
                    for c in range(2):
                        sp.dma_start(dst[:, c], mod_d[c, i].partition_broadcast(P)).then_inc(modv_in, 16)
                sp.dma_start(WR[:], w_router[0].rearrange("(k p) e -> p k e", p=P)).then_inc(wr_in, 16)
                for i, t in enumerate(ORDER):
                    if i >= 2:
                        sp.wait_ge(x1_made, i - 1)
                    sp.dma_start(XL[:, i % 2], x_rows[t]).then_inc(xl_in[i % 2], 16)
                for slot in range(4, 12):
                    expert_weights(sp, slot, 0)
                sp.wait_ge(mix_mm, 2 * TN)
                for slot in range(4):
                    expert_weights(sp, slot, 0)

            @block.gpsimd
            def _(pool):
                nc.gpsimd.memset(TA[:], 0.0).then_inc(ta_init, 1)
                nc.gpsimd.memset(POST[:], 0.0).then_inc(ta_init, 1)
                pool.wait_ge(ta_init, 2)
                for t in range(TN):
                    ins = nc.gpsimd.tensor_copy(TA[:, t, 0:NE, 0], CST[:, C_TOK + t:C_TOK + t + 1]
                                                .to_broadcast([P, NE]))
                ins.then_inc(ta_init, 1)
                for i, t in enumerate(ORDER):
                    c = 0 if t == CTX else 1
                    pool.wait_ge(x1_g, 2 * i + 2)
                    pool.wait_ge(xl_in[i % 2], 16 * (i // 2 + 1))
                    nc.gpsimd.tensor_tensor(X1[:, i % 2], X1[:, i % 2], XL[:, i % 2], ALU.add) \
                      .then_inc(x1_made, 1)
                    pool.wait_ge(x1_made, i + 1)
                    pool.dma_start(x1_d[t * P:(t + 1) * P, :], X1[:, i % 2]).then_inc(x1_out[i % 2], 16)
                    pool.wait_ge(h2_a, i + 1)
                    nc.gpsimd.tensor_tensor(H2[:, i % 2], H2[:, i % 2], SH2[:, c], ALU.add).then_inc(h2_made, 1)
                    pool.wait_ge(h2_made, i + 1)
                    pool.dma_start(h2_d[t * P:(t + 1) * P, :], H2[:, i % 2]).then_inc(h2_out[i % 2], 16)
                for s in (x1_out, h2_out):
                    pool.wait_ge(s[0], 80)
                    pool.wait_ge(s[1], 64)

            @block.tensor
            def _(pe):
                def mix_tile(i):
                    t = ORDER[i]
                    for h in range(2):
                        if i == 0:
                            for slot in (2 * h, 2 * h + 1):
                                pe.wait_ge(weights_in[slot], W_BASE + 16 * G + 16)
                        if i >= 2:
                            pe.wait_ge(x1_g, 2 * (i - 2) + h + 1)
                        for k in range(KT):
                            ins = nc.tensor.matmul(PS[2 * (i % 2) + h][:], MIX[:, k, t * P:(t + 1) * P],
                                                   W[:, 2 * h:2 * h + 2, k, :], start=(k == 0), stop=(k == KT - 1))
                        ins.then_inc(mix_mm, 1)

                def router_tile(i):
                    pe.wait_ge(h2_made, i + 1)
                    if i:
                        pe.wait_ge(h2_sb, 2 * i)
                    for h in range(2):
                        for k in range(4 * h, 4 * h + 4):
                            ins = nc.tensor.transpose(PS[4 + h][:, (k % 4) * P:(k % 4 + 1) * P],
                                                      H2[:, i % 2, k * P:(k + 1) * P], IDENT)
                        ins.then_inc(h2_t, 1)
                    pe.wait_ge(h2_sb, 2 * i + 2)
                    if i:
                        pe.wait_ge(lg_exp, i)
                    else:
                        pe.wait_ge(wr_in, 16)
                    for k in range(KT):
                        ins = nc.tensor.matmul(PS[6][:, 0:NE], H2T[:, k, :], WR[:, k, :], start=(k == 0),
                                               stop=(k == KT - 1))
                    ins.then_inc(logits, 1)

                def affinity_t(i):
                    t = ORDER[i]
                    pe.wait_ge(aff_made, i + 1)
                    if i:
                        pe.wait_ge(aft_made, i)
                    nc.tensor.transpose(PS[7][0:NE, 0:P], TA[:, t, 0:NE, 1], IDENT).then_inc(aff_t, 1)

                for i in range(TN + 2):
                    if i < TN:
                        mix_tile(i)
                    if 1 <= i <= TN:
                        router_tile(i - 1)
                    if i >= 2:
                        affinity_t(i - 2)
                pe.wait_ge(pos_made, 1)
                for t in range(TN):
                    ins = nc.tensor.transpose(PS[0][:, t * NE:(t + 1) * NE], CUM[:, t * P:(t + 1) * P],
                                              IDENT[0:NE, 0:NE])
                ins.then_inc(pos_t, 1)

            @block.scalar
            def _(act):
                for i in range(TN + 1):
                    if i < TN:
                        t = ORDER[i]
                        act.wait_ge(x1_made, i + 1)
                        if i:
                            act.wait_ge(n2_sq, i)
                        nc.scalar.activation(XJ2[:], X1[:, i % 2], ACT.Square,
                                             accum_out=RS2[:, 0, i:i + 1]).then_inc(n2_sq, 1)
                        act.wait_ge(n2_sq, i + 1)
                        nc.scalar.activation(RS2[:, 0, i:i + 1], RS2[:, 0, i:i + 1], ACT.Ln, bias=EPS,
                                             scale=1.0 / D).then_inc(n2_ln, 1)
                        act.wait_ge(n2_ln, i + 1)
                        nc.scalar.activation(RS2[:, 1, i:i + 1], RS2[:, 0, i:i + 1], ACT.Exp,
                                             scale=-0.5).then_inc(n2_rs, 1)
                    if i >= 1:
                        act.wait_ge(lg_max, i)
                        if i >= 3:
                            act.wait_ge(aff_made, i - 2)
                        nc.scalar.activation(LEX[:, (i - 1) % 2], PS[6][:, 0:NE], ACT.Exp,
                                             bias=SMX[:, 0, i - 1:i], accum_out=SMX[:, 1, i - 1:i]) \
                          .then_inc(lg_exp, 1)
                    if i < TN:
                        if i:
                            act.wait_ge(logits, i)
                        for h in range(2):
                            act.wait_ge(h2_t, 2 * i + h + 1)
                            nc.scalar.activation(H2T[:, 4 * h:4 * h + 4, :].rearrange("p k n -> p (k n)"),
                                                 PS[4 + h][:], ACT.Copy).then_inc(h2_sb, 1)

            @block.vector
            def _(dve):
                def residual(i):
                    c = 0 if ORDER[i] == CTX else 1
                    if i == 0:
                        dve.wait_ge(modv_in, 96)
                    for h in range(2):
                        dve.wait_ge(mix_mm, 2 * i + h + 1)
                        if i >= 2 and h == 0:
                            dve.wait_ge(x1_out[i % 2], 16 * (i // 2))
                            dve.wait_ge(n2_sq, i - 1)
                        cols = slice(512 * h, 512 * h + 512)
                        nc.vector.tensor_tensor(X1[:, i % 2, cols], PS[2 * (i % 2) + h][:], G1[:, c, cols],
                                                ALU.mult).then_inc(x1_g, 1)

                def scaled(i):
                    c = 0 if ORDER[i] == CTX else 1
                    dve.wait_ge(n2_rs, i + 1)
                    if i >= 2:
                        dve.wait_ge(h2_out[i % 2], 16 * (i // 2))
                        dve.wait_ge(h2_t, 2 * (i - 1))
                    nc.vector.scalar_tensor_tensor(H2[:, i % 2], X1[:, i % 2], RS2[:, 1, i:i + 1], A2[:, c],
                                                   ALU.mult, ALU.mult).then_inc(h2_a, 1)

                def softmax_max(i):
                    dve.wait_ge(logits, i + 1)
                    nc.vector.tensor_reduce(SMX[:, 0, i:i + 1], PS[6][:, 0:NE], AX.X, ALU.max,
                                            negate=True).then_inc(lg_max, 1)

                def softmax_end(i):
                    dve.wait_ge(lg_exp, i + 1)
                    nc.vector.reciprocal(SMX[:, 2, i:i + 1], SMX[:, 1, i:i + 1]).then_inc(lg_rec, 1)
                    dve.wait_ge(lg_rec, i + 1)
                    if i == 0:
                        dve.wait_ge(ta_init, 3)
                    nc.vector.tensor_scalar(TA[:, ORDER[i], 0:NE, 1], LEX[:, i % 2], SMX[:, 2, i:i + 1], None,
                                            ALU.mult).then_inc(aff_made, 1)

                def affinity_rows(i):
                    t = ORDER[i]
                    dve.wait_ge(aff_t, i + 1)
                    nc.vector.tensor_copy(AFT[:, t * P:(t + 1) * P], PS[7][0:NE, 0:P]).then_inc(aft_made, 1)

                n = [0]

                def chained(ins):
                    ins.then_inc(topk, 1)
                    n[0] += 1
                    dve.wait_ge(topk, n[0])

                def select(lo_, hi_, cap):
                    chained(nc.vector.tensor_copy(WK[:, lo_:hi_], AFT[:, lo_:hi_]))
                    for r in range(cap // 8):
                        chained(nc.vector.max(M8[:, r % 2], WK[:, lo_:hi_]))
                        chained(nc.vector.match_replace(WK[:, lo_:hi_], M8[:, r % 2], WK[:, lo_:hi_], -1.0))
                    chained(nc.vector.tensor_scalar(SEL[:, lo_:hi_], WK[:, lo_:hi_], 0.0, None, ALU.is_lt))
                    chained(nc.vector.tensor_tensor_scan(CUM[:, lo_:hi_], SEL[:, lo_:hi_], SEL[:, lo_:hi_],
                                                         0.0, ALU.add, ALU.max))

                for i in range(TN + 2):
                    if 1 <= i <= TN:
                        scaled(i - 1)
                    if i < TN:
                        residual(i)
                    if i >= 1 and i <= TN:
                        softmax_max(i - 1)
                        softmax_end(i - 1)
                    if i >= 2:
                        affinity_rows(i - 2)
                dve.wait_ge(aft_made, TN)
                dve.wait_ge(mix_mm, 2 * TN)
                select(TL * P, T, CAP_C)
                select(0, TL * P, CAP_L)
                nc.vector.tensor_tensor(CUM[:], CUM[:], SEL[:], ALU.mult).then_inc(pos_made, 1)
                dve.wait_ge(pos_t, 1)
                nc.vector.tensor_copy(POST[:, :, 0:NE], PS[0][:, 0:TN * NE].rearrange("p (t e) -> p t e", t=TN)) \
                  .then_inc(post_made, 1)

        if upto == "mixing":
            return

        next_stage()

        NX = CAP_L + CAP_C
        ex = Region(nc, after_ta, hi)
        G2 = ex("G2", [P, 2, D])
        OH = ex("OH", [P, TN, P])
        IDX = ex("IDX", [P, 2, 2], U32)
        TW = ex("TW", [P, 2, 2])
        XG = ex("XG", [P, D])
        XC = ex("XC", [CAP_C, D])
        XET = ex("XET", [P, KT, NX])
        SG = ex("SG", [P, 2, NX])
        GU = ex("GU", [P, 2, NX])
        HID = ex("HID", [P, KT, NX])
        YT = ex("YT", [P, 2, 4, NX])
        YS = ex("YS", [P, D])
        YC = ex("YC", [CAP_C, D])

        g2_in = sem("g2_in")
        oh_made = sem("oh_made")
        place = sem("place")
        idx_made = sem("idx_made")
        xg_in = sem("xg_in")
        x_t = sem("x_t")
        xet_made = sem("xet_made")
        gate_mm = sem("gate_mm")
        up_mm = sem("up_mm")
        g_exp = sem("g_exp")
        g_ln = sem("g_ln")
        g_sig = sem("g_sig")
        g_silu = sem("g_silu")
        hid = sem("hid")
        down_mm = sem("down_mm")
        yt_made = sem("yt_made")
        y_t = sem("y_t")
        ys_made = sem("ys_made")
        y_out = sem("y_out")

        with nc.Block() as block:
            @block.sync
            def _(sp):
                for c in range(2):
                    sp.dma_start(G2[:, c], mod_d[c, 3].partition_broadcast(P)).then_inc(g2_in, 16)
                with sp.Fori(0, NE - 1) as e:
                    for slot in range(4, 12):
                        mm, c = (gate_mm, slot - 4) if slot < 8 else (up_mm, slot - 8)
                        sp.wait_ge(mm, e * KT + 2 * c + 2)
                        settled(sp)
                        expert_weights(sp, slot, e + 1)
                    for slot in range(4):
                        sp.wait_ge(down_mm, e * KT + 2 * slot + 2)
                        settled(sp)
                        expert_weights(sp, slot, e + 1)

            def fetch(pool, e, r):
                pool.wait_ge(idx_made, e + 1)
                pool.wait_ge(x_t, 3 * e)
                settled(pool)
                pool.indirect_dma_start(XG[:], None, h2_d, bass.IndirectOffsetOnAxis(IDX[:, 0, r:r + 1], 0)) \
                    .then_inc(xg_in, 16)
                pool.indirect_dma_start(XC[:], None, h2_d,
                                        bass.IndirectOffsetOnAxis(IDX[0:CAP_C, 1, r:r + 1], 0)) \
                    .then_inc(xg_in, 16)

            def add_rows(pool, e, r):
                pool.wait_ge(ys_made, e * 4 + 4)
                pool.wait_ge(y_out, e * 32)
                settled(pool)
                pool.indirect_dma_start(x1_d, bass.IndirectOffsetOnAxis(IDX[:, 0, r:r + 1], 0), YS[:], None,
                                        compute_op=ALU.add).then_inc(y_out, 16)
                pool.indirect_dma_start(x1_d, bass.IndirectOffsetOnAxis(IDX[0:CAP_C, 1, r:r + 1], 0), YC[:],
                                        None, compute_op=ALU.add).then_inc(y_out, 16)

            @block.gpsimd
            def _(pool):
                fetch(pool, 0, 0)
                with pool.Fori(0, NE // 2) as h:
                    for r in range(2):
                        e = 2 * h + r
                        fetch(pool, e + 1, 1 - r)
                        add_rows(pool, e, r)
                pool.wait_ge(y_out, NE * 32)
                pool.wait_ge(xg_in, (NE + 1) * 32)

            @block.tensor
            def _(pe):
                def places(e):
                    pe.wait_ge(oh_made, e + 1)
                    if not isinstance(e, int):
                        pe.wait_ge(ys_made, e * 4 - 4)
                    for t in range(TL):
                        nc.tensor.matmul(PS[7][:, 0:2], OH[:, t, :], TA[:, t, ds(e, 1), :].rearrange("p a c -> p (a c)"),
                                         start=(t == 0), stop=(t == TL - 1))
                    nc.tensor.matmul(PS[7][0:CAP_C, 2:4], OH[:, CTX, 0:CAP_C],
                                     TA[:, CTX, ds(e, 1), :].rearrange("p a c -> p (a c)"),
                                     start=True, stop=True).then_inc(place, 1)

                def rows_t(e):
                    pe.wait_ge(xg_in, e * 32 + 32)
                    if not isinstance(e, int):
                        pe.wait_ge(xet_made, e * 3)
                        pe.wait_ge(ys_made, e * 4 - 4)
                    for h in range(2):
                        for k in range(4 * h, 4 * h + 4):
                            ins = nc.tensor.transpose(PS[4 + h][:, (k % 4) * P:(k % 4 + 1) * P],
                                                      XG[:, k * P:(k + 1) * P], IDENT)
                        ins.then_inc(x_t, 1)
                    for k in range(KT):
                        ins = nc.tensor.transpose(PS[6][:, k * CAP_C:(k + 1) * CAP_C], XC[:, k * P:(k + 1) * P],
                                                  IDENT[0:CAP_C, 0:CAP_C])
                    ins.then_inc(x_t, 1)

                def results_t(e, h):
                    pe.wait_ge(yt_made, e * KT + 4 * h + 4)
                    pe.wait_ge(idx_made, e + 2)
                    pe.wait_ge(xet_made, e * 3 + 6)
                    for q, (bank, rows) in enumerate(((7, slice(0, CAP_L)), (6, slice(CAP_L, NX)))):
                        n = rows.stop - rows.start
                        if h:
                            pe.wait_ge(ys_made, e * 4 + 1 + q)
                        for f in range(4):
                            ins = nc.tensor.transpose(PS[bank][0:n, f * P:(f + 1) * P], YT[:, h, f, rows], IDENT)
                        ins.then_inc(y_t, 1)

                places(0)
                rows_t(0)
                with pe.Fori(0, NE) as e:
                    for f in range(KT):
                        for s, mm in ((0, gate_mm), (1, up_mm)):
                            if f == 0:
                                if s == 0:
                                    pe.wait_ge(xet_made, e * 3 + 3)
                            if f % 2 == 0:
                                pe.wait_ge(we_in[4 + 4 * s + f // 2], e * 16 + 16)
                            if f < 2:
                                pe.wait_ge(yt_made, e * KT)
                            elif s == 0:
                                pe.wait_ge(g_silu, e * KT + f - 1)
                            else:
                                pe.wait_ge(hid, e * KT + f - 1)
                            for k in range(KT):
                                ins = nc.tensor.matmul(PS[2 * s + f % 2][:, 0:NX],
                                                       WE[:, 4 + 4 * s + f // 2, k, (f % 2) * P:(f % 2 + 1) * P],
                                                       XET[:, k, :], start=(k == 0), stop=(k == KT - 1))
                            ins.then_inc(mm, 1)
                        if f == 3:
                            places(e + 1)
                    rows_t(e + 1)
                    for f in range(KT):
                        if f % 2 == 0:
                            pe.wait_ge(we_in[f // 2], e * 16 + 16)
                        if f == 0:
                            pe.wait_ge(hid, e * KT + KT)
                        if f >= 4:
                            pe.wait_ge(yt_made, e * KT + f - 3)
                        for k in range(KT):
                            ins = nc.tensor.matmul(PS[f % 4][:, 0:NX], WE[:, f // 2, k, (f % 2) * P:(f % 2 + 1) * P],
                                                   HID[:, k, :], start=(k == 0), stop=(k == KT - 1))
                        ins.then_inc(down_mm, 1)
                        if f == 5:
                            results_t(e, 0)
                    results_t(e, 1)

            @block.scalar
            def _(act):
                with act.Fori(0, NE) as e:
                    for f in range(KT):
                        n = e * KT + f
                        b = SG[:, f % 2]
                        act.wait_ge(gate_mm, n + 1)
                        act.wait_ge(g_silu, e * KT + (f - 1 if f >= 2 else 0))
                        nc.scalar.activation(b, PS[f % 2][:, 0:NX], ACT.Exp, scale=-1.0).then_inc(g_exp, 1)
                        act.wait_ge(g_exp, n + 1)
                        nc.scalar.activation(b, b, ACT.Ln, bias=1.0).then_inc(g_ln, 1)
                        act.wait_ge(g_ln, n + 1)
                        nc.scalar.activation(b, b, ACT.Exp, scale=-1.0).then_inc(g_sig, 1)
                    for f in range(KT):
                        act.wait_ge(down_mm, e * KT + f + 1)
                        act.wait_ge(y_t, e * 4)
                        nc.scalar.activation(YT[:, f // 4, f % 4], PS[f % 4][:, 0:NX], ACT.Copy).then_inc(yt_made, 1)

            @block.vector
            def _(dve):
                def one_hot(e):
                    dve.wait_ge(place, e)
                    for t in range(TN):
                        ins = nc.vector.tensor_scalar(OH[:, t], CST[:, C_IOTA:C_IOTA + P], POST[:, t, ds(e, 1)], None,
                                                      ALU.is_equal)
                    ins.then_inc(oh_made, 1)

                def places(e, r):
                    dve.wait_ge(place, e + 1)
                    if not isinstance(e, int):
                        dve.wait_ge(y_out, e * 32 - 32)
                    nc.vector.tensor_copy(TW[:, 0, r:r + 1], PS[7][:, 1:2])
                    nc.vector.tensor_copy(TW[0:CAP_C, 1, r:r + 1], PS[7][0:CAP_C, 3:4])
                    nc.vector.tensor_copy(IDX[:, 0, r:r + 1], PS[7][:, 0:1])
                    nc.vector.tensor_copy(IDX[0:CAP_C, 1, r:r + 1], PS[7][0:CAP_C, 2:3]).then_inc(idx_made, 1)

                def rows(e):
                    dve.wait_ge(x_t, e * 3 + 1)
                    dve.wait_ge(up_mm, e * KT)
                    nc.vector.tensor_copy(XET[:, 0:4, 0:CAP_L], PS[4][:].rearrange("p (k n) -> p k n", k=4)) \
                      .then_inc(xet_made, 1)
                    dve.wait_ge(x_t, e * 3 + 2)
                    nc.vector.tensor_copy(XET[:, 4:8, 0:CAP_L], PS[5][:].rearrange("p (k n) -> p k n", k=4)) \
                      .then_inc(xet_made, 1)
                    dve.wait_ge(x_t, e * 3 + 3)
                    nc.vector.tensor_copy(XET[:, :, CAP_L:NX],
                                          PS[6][:, 0:KT * CAP_C].rearrange("p (k n) -> p k n", k=KT)) \
                      .then_inc(xet_made, 1)

                def results(e, h, r):
                    cols = slice(512 * h, 512 * h + 512)
                    for q, (bank, n, dst, c) in enumerate(((7, CAP_L, YS, 1), (6, CAP_C, YC, 0))):
                        dve.wait_ge(y_t, e * 4 + 2 * h + q + 1)
                        if h == 0 and q == 0:
                            dve.wait_ge(y_out, e * 32)
                        nc.vector.scalar_tensor_tensor(dst[0:n, cols], PS[bank][0:n, :], TW[0:n, q, r:r + 1],
                                                       G2[0:n, c, cols], ALU.mult, ALU.mult).then_inc(ys_made, 1)

                one_hot(0)
                places(0, 0)
                rows(0)
                dve.wait_ge(g2_in, 32)
                with dve.Fori(0, NE // 2) as hh:
                    for r in range(2):
                        e = 2 * hh + r
                        one_hot(e + 1)
                        for f in range(KT):
                            n = e * KT + f
                            dve.wait_ge(g_sig, n + 1)
                            dve.wait_ge(hid, n - 1 if f >= 1 else n)
                            nc.vector.tensor_tensor(GU[:, f % 2], SG[:, f % 2], PS[f % 2][:, 0:NX], ALU.mult) \
                              .then_inc(g_silu, 1)
                            dve.wait_ge(g_silu, n + 1)
                            dve.wait_ge(up_mm, n + 1)
                            if f == 0:
                                dve.wait_ge(down_mm, e * KT)
                            nc.vector.tensor_tensor(HID[:, f], GU[:, f % 2], PS[2 + f % 2][:, 0:NX], ALU.mult) \
                              .then_inc(hid, 1)
                            if f == 5:
                                places(e + 1, 1 - r)
                        rows(e + 1)
                        for h in range(2):
                            results(e, h, r)

        next_stage()

        fn = Region(nc, after_ta, hi)
        FN = fn("FN", [P, D])
        XF = fn("XF", [P, 4, D])
        YF = fn("YF", [P, 3, D])
        XJ3 = fn("XJ3", [P, D])
        RS3 = fn("RS3", [P, 2, TN])
        fn_in = sem("fn_in")
        xf_in = [sem(f"xf_in{i}") for i in range(4)]
        f_sq = sem("f_sq")
        f_ln = sem("f_ln")
        f_rs = sem("f_rs")
        f_out = sem("f_out")
        y_stored = [sem(f"y_stored{i}") for i in range(3)]
        y_rows = [y_sample[0, t * P:(t + 1) * P, :] for t in range(TL)] + [y_prompt[0]]

        with nc.Block() as block:
            @block.sync
            def _(sp):
                sp.dma_start(FN[:], final_norm.partition_broadcast(P)).then_inc(fn_in, 16)
                for t in range(TN):
                    if t >= 4:
                        sp.wait_ge(f_out, t - 3)
                    sp.dma_start(XF[:, t % 4], x1_d[t * P:(t + 1) * P, :]).then_inc(xf_in[t % 4], 16)

            @block.scalar
            def _(act):
                for t in range(TN):
                    act.wait_ge(xf_in[t % 4], 16 * (t // 4 + 1))
                    if t:
                        act.wait_ge(f_sq, t)
                    nc.scalar.activation(XJ3[:], XF[:, t % 4], ACT.Square,
                                         accum_out=RS3[:, 0, t:t + 1]).then_inc(f_sq, 1)
                    act.wait_ge(f_sq, t + 1)
                    nc.scalar.activation(RS3[:, 0, t:t + 1], RS3[:, 0, t:t + 1], ACT.Ln, bias=EPS,
                                         scale=1.0 / D).then_inc(f_ln, 1)
                    act.wait_ge(f_ln, t + 1)
                    nc.scalar.activation(RS3[:, 1, t:t + 1], RS3[:, 0, t:t + 1], ACT.Exp,
                                         scale=-0.5).then_inc(f_rs, 1)

            @block.vector
            def _(dve):
                dve.wait_ge(fn_in, 16)
                for t in range(TN):
                    dve.wait_ge(f_rs, t + 1)
                    if t >= 3:
                        dve.wait_ge(y_stored[t % 3], 16 * (t // 3))
                    nc.vector.scalar_tensor_tensor(YF[:, t % 3], XF[:, t % 4], RS3[:, 1, t:t + 1], FN[:],
                                                   ALU.mult, ALU.mult).then_inc(f_out, 1)

            @block.gpsimd
            def _(pool):
                for t in range(TN):
                    pool.wait_ge(f_out, t + 1)
                    pool.dma_start(y_rows[t], YF[:, t % 3]).then_inc(y_stored[t % 3], 16)
                for i in range(3):
                    pool.wait_ge(y_stored[i], 48)


_INS = ['x_prompt', 'x_sample', 'state_hgrn', 'c', 'c_ctx', 'w_ada', 'b_ada', 'norm1', 'w_in', 'conv_w', 'conv_b',
        'hgrn_lb', 'hgrn_onorm', 'w_out_a', 'w_out_b', 'w_o', 'norm2', 'w_router', 'w_e_gate', 'w_e_up',
        'w_e_down', 'final_norm']
_OUTS = [((1, P, D), 'float32'), ((1, TL * P, D), 'float32'), ((1, 1, 2, D // P, P, P), 'float32')]


def kernel(**inputs):
    import numpy as _np
    import concourse.bacc as _bacc
    from concourse import mybir as _mybir
    from concourse.bass_utils import run_bass_kernel_spmd as _run

    nc = _bacc.Bacc("TRN2", target_bir_lowering=False, num_devices=1)
    arrays = {f"in_{name}_dram": _np.ascontiguousarray(inputs[name]) for name in _INS}
    arrays["in_shape_constants_dram"] = shape_constants()
    args = [nc.dram_tensor(name, a.shape, _mybir.dt.from_np(a.dtype), kind="ExternalInput").ap()
            for name, a in arrays.items()]
    for i, (shape, dtype) in enumerate(_OUTS):
        dt = _mybir.dt.from_np(_np.dtype(dtype))
        args.append(nc.dram_tensor(f"out_{i}_dram", shape, dt, kind="ExternalOutput").ap())
    trunk(nc, *args)
    r = _run(nc, [arrays], core_ids=[0])
    return tuple(r.results[0][f"out_{i}_dram"] for i in range(len(_OUTS)))
```

```python
from contextlib import ExitStack

import numpy as np

import concourse.bass as bass
from concourse import mybir
from concourse.alu_op_type import AluOpType as ALU

ACT = mybir.ActivationFunctionType
AX = mybir.AxisListType
F32 = mybir.dt.float32
F32R = mybir.dt.float32r
U32 = mybir.dt.uint32
ds = bass.ds

P = 128
D = 1024
KT = D // P
TL = 8
TN = TL + 1
CTX = TL
T = TN * P
NCH = 3
CH = T // NCH
ROW = 64
NH = 8
GW = 256
NE = 16
CAP_L = 2 * TL * P // NE
CAP_C = 2 * P // NE
EPS = 1e-6
PARTS = [(0, 0), (1, 0), (0, 1)]
SPLIT_AT_Z = {1: [0], 3: [1]}
SPLIT_AT_1 = {1: [2], 2: [3], 3: [4], 7: [5]}
SPLIT_AT_2 = {0: [6], 5: [7], 6: [8], 7: [9]}
W_SPLIT = 10 * NH

C_ID = 0
C_ST = C_ID + P
C_MK = C_ST + 2 * P
C_ONE = C_MK + 2 * P
C_IOTA = C_ONE + 1
C_TOK = C_IOTA + P
C_ML = C_TOK + TN
C_END = C_ML + 2 * 4 * P


def shape_constants():
    c = np.zeros((P, C_END), np.float32)
    s, t = np.arange(P)[:, None], np.arange(P)[None, :]
    c[:, C_ID:C_ID + P] = s == t
    edge = (s <= t).astype(np.float32)

    def about(size, mid):
        same = s // size == t // size
        return same, ((t % size >= mid) & (s % size >= mid) & (s <= t) & same,
                      (t % size < mid) & (s % size < mid) & (s > t) & same)

    _, (after, before) = about(32, 16)
    near = after.astype(np.float32) - before
    _, (after, before) = about(128, 64)
    half = (after | before).astype(np.float32)
    _, (after, before) = about(64, 32)
    quarter = (after | before).astype(np.float32)
    fwd = [edge, near, half, quarter]
    for i, m in enumerate(fwd):
        c[:, C_ML + i * P:C_ML + (i + 1) * P] = m
        c[:, C_ML + (4 + i) * P:C_ML + (5 + i) * P] = m[::-1, ::-1]
    c[:, C_ST:C_ST + P] = s > t
    c[:, C_ST + P:C_ST + 2 * P] = s < t
    c[:, C_MK:C_MK + P] = s <= t
    c[:, C_MK + P:C_MK + 2 * P] = s >= t
    c[:, C_ONE] = 1
    c[:, C_IOTA:C_IOTA + P] = t + 1
    c[:, C_TOK:C_TOK + TN] = np.arange(P)[:, None] + P * np.arange(TN)[None, :]
    return c


class Region:

    def __init__(self, nc, start, end):
        self.nc, self.at, self.end = nc, start, end

    def __call__(self, name, shape, dtype=F32):
        size = int(np.prod(shape[1:])) * 4
        t = self.nc.alloc_sbuf_tensor_at(name, shape, dtype, offset=self.at)
        self.at += (size + 31) // 32 * 32
        assert self.at <= self.end, (name, self.at, self.end)
        return t


def trunk(nc, x_prompt, x_sample, state, cond, c_ctx, w_ada, b_ada, norm1, w_in, conv_w, conv_b,
          hgrn_lb, onorm, w_out_a, w_out_b, w_o, norm2, w_router, w_eg, w_eu, w_ed, final_norm,
          consts, y_prompt, y_sample, new_state, upto="all"):
    ctx = ExitStack()
    with ctx:
        stage_sems = []

        def lasting(name):
            return nc.alloc_semaphore(name)

        def sem(name):
            stage_sems.append(nc.alloc_semaphore(name))
            return stage_sems[-1]

        def next_stage():
            nc.clear_and_free_semaphores(list(stage_sems))
            stage_sems.clear()
            nc.all_engine_barrier()

        def scratch(name, shape):
            return nc.dram_tensor(name, shape, F32, kind="Internal").ap()

        mod_d = scratch("mod_d", [2, 4, D])
        lb_d = scratch("lb_d", [2, 2, D])
        ya_d = scratch("ya_d", [D, T])
        ob_d = scratch("ob_d", [D, T])
        sg_d = scratch("sg_d", [2, D, T])
        sg_flat = sg_d.rearrange("a d t -> (a d) t")
        x1_d = scratch("x1_d", [T, D])
        h2_d = scratch("h2_d", [T, D])

        PS = [ctx.enter_context(nc.psum_tensor(f"bank{i}", [P, 512], F32)) for i in range(8)]

        lo = (nc.sbuf_base + 63) // 64 * 64
        hi = nc.sbuf_top // 64 * 64
        keep = Region(nc, lo, hi)
        CST = keep("CST", [P, C_ML])
        MLR = keep("MLR", [P, 2, 4 * P], F32R)
        IDENT = CST[:, C_ID:C_ID + P]
        ONE = CST[:, C_ONE:C_ONE + 1]
        A1T = keep("A1T", [P, KT, 2])
        SH1T = keep("SH1T", [P, KT, 2])
        CW = keep("CW", [P, KT, 5])
        CT = keep("CT", [P, KT, 2])
        W_OFF = keep.at
        W = keep("W", [P, 5, 2, KT, P], F32R)
        W_FULL = nc.alloc_sbuf_tensor_at("W_FULL", [P, 5, 2, KT, P], F32, offset=W_OFF)
        HT_OFF = keep.at
        HT = keep("HT", [P, 2, KT, T], F32R)
        HT_FULL = nc.alloc_sbuf_tensor_at("HT_FULL", [P, 2, KT, T], F32, offset=HT_OFF)
        after_h = keep.at
        we_in = [lasting(f"we_in{i}") for i in range(12)]

        const_in = lasting("const_in")

        passed = {e: lasting(f"passed_{e}") for e in ("sp", "pool")}

        def settled(eng):
            eng.sem_inc(passed["pool" if eng is nc.gpsimd else "sp"], 1)

        weights_in = [lasting(f"weights_in{i}") for i in range(5)]
        wo_in = lasting("wo_in")
        w_hi = lasting("w_hi")
        w_lo = lasting("w_lo")

        SLOT = KT * GW * 4
        WEA = nc.alloc_sbuf_tensor_at("WEA", [P, 8, KT, GW], F32, offset=W_OFF)
        WED_OFF = HT_OFF + KT * T * 4
        WED = nc.alloc_sbuf_tensor_at("WED", [P, 4, KT, GW], F32, offset=WED_OFF)

        pro = Region(nc, after_h, hi)
        early = Region(nc, W_OFF + 3 * 2 * KT * P * 4, HT_OFF)
        MLF = early("MLF", [P, 2, 4 * P])
        CWR = early("CWR", [5, D])
        AW = pro("AW", [P, 2, KT, 512])
        CR = early("CR", [2, D])
        CE = early("CE", [2, D])
        MODR = pro("MODR", [2, 6 * D])
        NR = pro("NR", [2, 2, D])
        LBI = pro("LBI", [16, 2, P])
        LBM = pro("LBM", [16, P])
        LBO = pro("LBO", [16, 2, P])
        LBS = pro("LBS", [16, P])
        XT = pro("XT", [P, 2, D])
        XJ = pro("XJ", [P, D])
        XN = pro("XN", [P, 2, D])
        XS = pro("XS", [P, TN])
        XR = pro("XR", [P, TN])
        ADA = 12 - 2
        w_ada_v = w_ada[0].rearrange("(k p) n -> p k n", p=P)
        x_rows = [x_sample[0, t * P:(t + 1) * P, :] for t in range(TL)] + [x_prompt[0]]

        cond_in = sem("cond_in")
        rows_in = sem("rows_in")
        lbi_in = sem("lbi_in")
        ada_in = [sem(f"ada_in{i}") for i in range(2)]
        x_in_s = [sem(f"x_in{i}") for i in range(2)]
        ml_in = sem("ml_in")
        ml_made = sem("ml_made")
        cond_act = sem("cond_act")
        cond_silu = sem("cond_silu")
        cond_t = sem("cond_t")
        cond_ct = sem("cond_ct")
        ada_mm = sem("ada_mm")
        ada_row = sem("ada_row")
        mod_fix = sem("mod_fix")
        mod_t = sem("mod_t")
        mod_ct = sem("mod_ct")
        mod_out = sem("mod_out")
        lb_step = sem("lb_step")
        lb_exp = sem("lb_exp")
        lb_out = sem("lb_out")
        sq_done = sem("sq_done")
        rs_ln = sem("rs_ln")
        rs_done = sem("rs_done")
        xn_done = sem("xn_done")
        ht_t = sem("ht_t")
        ht_dve = sem("ht_dve")
        ht_act = sem("ht_act")
        ht_hi = sem("ht_hi")
        ht_lo = sem("ht_lo")

        w_in_v = w_in[0].rearrange("(k p) n -> p k n", p=P)
        XI, BG, CG, Q, ZF, ZB, IV, OG, GA, GB = (i * D for i in range(10))

        def wload(eng, slot, src, col):
            eng.dma_start(W_FULL[:, slot, 1], src[:, :, ds(col, P)]).then_inc(weights_in[slot], 16)

        def evac_h(eng, t, half):
            c = 0 if t == CTX else 1
            eng.wait_ge(mod_ct, 1)
            eng.wait_ge(ht_t, 2 * t + half + 1)
            for k in range(4 * half, 4 * half + 4):
                out = HT_FULL[:, 1, k, t * P:(t + 1) * P]
                src = PS[4 + half + 2 * (t % 2)][:, (k % 4) * P:(k % 4 + 1) * P]
                if half == 0:
                    ins = nc.vector.tensor_scalar(out, src, A1T[:, k, c:c + 1],
                                                  SH1T[:, k, c:c + 1], ALU.mult, ALU.add)
                else:
                    ins = nc.scalar.activation(out, src, ACT.Identity, bias=SH1T[:, k, c:c + 1],
                                               scale=A1T[:, k, c:c + 1])
            ins.then_inc(ht_act if half else ht_dve, 1)

        def h_high(t):
            nc.scalar.wait_ge(ht_dve, t + 1)
            nc.scalar.wait_ge(ht_act, t + 1)
            cols = slice(t * P, (t + 1) * P)
            nc.scalar.activation(HT[:, 0, :, cols], HT_FULL[:, 1, :, cols], ACT.Copy).then_inc(ht_hi, 1)

        def h_low(t):
            nc.vector.wait_ge(ht_hi, t + 1)
            cols = slice(t * P, (t + 1) * P)
            nc.vector.tensor_tensor(HT[:, 1, :, cols], HT_FULL[:, 1, :, cols],
                                    HT[:, 0, :, cols].bitcast(F32), ALU.subtract).then_inc(ht_lo, 1)

        with nc.Block() as block:
            @block.sync
            def _(sp):
                sp.dma_start(CR[0:1, :], c_ctx.rearrange("(a n) -> a n", a=1)).then_inc(cond_in, 16)
                sp.dma_start(CR[1:2, :], cond).then_inc(cond_in, 16)
                for d in range(2):
                    sp.dma_start(LBI[8 * d:8 * d + 8], hgrn_lb[d].rearrange("j (c f) -> c j f", f=P)) \
                      .then_inc(lbi_in, 16)
                sp.dma_start(CST[:], consts[:, 0:C_ML]).then_inc(const_in, 16)
                for i in range(2):
                    sp.dma_start(AW[:, i], w_ada_v[:, :, i * 512:(i + 1) * 512]).then_inc(ada_in[i], 16)
                sp.dma_start(MODR[:], b_ada[0].partition_broadcast(2)).then_inc(rows_in, 16)
                sp.dma_start(NR[:, 0, :], norm1[0].partition_broadcast(2)).then_inc(rows_in, 16)
                sp.dma_start(NR[:, 1, :], norm2[0].partition_broadcast(2)).then_inc(rows_in, 16)
                sp.dma_start(MLF[:].rearrange("p d n -> p (d n)"), consts[:, C_ML:C_END]).then_inc(ml_in, 16)
                for b in range(2, ADA):
                    sp.wait_ge(ada_mm, b - 1)
                    sp.dma_start(AW[:, b % 2], w_ada_v[:, :, b * 512:(b + 1) * 512]).then_inc(ada_in[b % 2], 16)
                    if b == 9:
                        sp.wait_ge(ml_made, 1)
                        sp.wait_ge(cond_ct, 1)
                        for slot, off in enumerate((ZF, ZB, IV)):
                            wload(sp, slot, w_in_v, off)
                for slot, off in ((3, Q), (4, OG)):
                    wload(sp, slot, w_in_v, off)
                sp.wait_ge(mod_out, 48)
                sp.wait_ge(lb_out, 64)

            @block.scalar
            def _(act):
                act.preload_act_table_set("natural_log_exp_and_others")
                act.dma_start(CWR[0:3, :], conv_w[0]).then_inc(const_in, 16)
                act.dma_start(CWR[3:4, :], conv_b).then_inc(const_in, 16)
                act.dma_start(CWR[4:5, :], onorm).then_inc(const_in, 16)
                act.wait_ge(cond_in, 32)
                nc.scalar.activation(CE[:], CR[:], ACT.Exp, scale=-1.0).then_inc(cond_act, 1)
                act.wait_ge(cond_act, 1)
                nc.scalar.activation(CE[:], CE[:], ACT.Ln, bias=1.0).then_inc(cond_act, 1)
                act.wait_ge(cond_act, 2)
                nc.scalar.activation(CE[:], CE[:], ACT.Exp, scale=-1.0).then_inc(cond_act, 1)
                act.wait_ge(lb_step, 3)
                nc.scalar.activation(LBI[:], LBI[:], ACT.Exp).then_inc(lb_exp, 1)
                for t in range(TN + 1):
                    if t < TN:
                        act.wait_ge(x_in_s[t % 2], 16 * (t // 2 + 1))
                        if t:
                            act.wait_ge(sq_done, t)
                        nc.scalar.activation(XJ[:], XT[:, t % 2], ACT.Square,
                                             accum_out=XS[:, t:t + 1]).then_inc(sq_done, 1)
                        act.wait_ge(sq_done, t + 1)
                        nc.scalar.activation(XS[:, t:t + 1], XS[:, t:t + 1], ACT.Ln, bias=EPS,
                                             scale=1.0 / D).then_inc(rs_ln, 1)
                        act.wait_ge(rs_ln, t + 1)
                        nc.scalar.activation(XR[:, t:t + 1], XS[:, t:t + 1], ACT.Exp,
                                             scale=-0.5).then_inc(rs_done, 1)
                    if t > 0:
                        evac_h(act, t - 1, 1)
                    if t > 1:
                        h_high(t - 2)
                    if t == TN - 1:
                        for slot in range(3):
                            act.wait_ge(weights_in[slot], 16)
                            nc.scalar.activation(W[:, slot, 0], W_FULL[:, slot, 1], ACT.Copy).then_inc(w_hi, 1)
                h_high(TN - 1)

            @block.tensor
            def _(pe):
                pe.wait_ge(const_in, 64)
                pe.wait_ge(cond_silu, 1)
                for k in range(KT):
                    ins = nc.tensor.transpose(PS[0][:, 2 * k:2 * k + 2], CR[:, k * P:(k + 1) * P],
                                              IDENT[0:2, 0:2])
                for k in range(KT):
                    ins = nc.tensor.transpose(PS[0][:, 16 + 5 * k:21 + 5 * k], CWR[:, k * P:(k + 1) * P],
                                              IDENT[0:5, 0:5])
                ins.then_inc(cond_t, 1)
                pe.wait_ge(cond_ct, 1)
                def ada(b):
                    pe.wait_ge(ada_in[b % 2], 16 * (b // 2 + 1))
                    if b >= 2:
                        pe.wait_ge(ada_row, b - 1)
                    for k in range(KT):
                        ins = nc.tensor.matmul(PS[1 + b % 2][0:2, :], CT[:, k, :], AW[:, b % 2, k, :],
                                               start=(k == 0), stop=(k == KT - 1))
                    ins.then_inc(ada_mm, 1)

                for b in range(4):
                    ada(b)
                pe.wait_ge(mod_fix, 1)
                for k in range(KT):
                    nc.tensor.transpose(PS[3][:, 2 * k:2 * k + 2], MODR[:, k * P:(k + 1) * P],
                                        IDENT[0:2, 0:2])
                    ins = nc.tensor.transpose(PS[3][:, 16 + 2 * k:18 + 2 * k],
                                              MODR[:, D + k * P:D + (k + 1) * P], IDENT[0:2, 0:2])
                ins.then_inc(mod_t, 1)
                for t in range(TN):
                    pe.wait_ge(xn_done, t + 1)
                    for half in range(2):
                        if t >= 2:
                            pe.wait_ge(ht_act if half else ht_dve, t - 1)
                        for k in range(4 * half, 4 * half + 4):
                            ins = nc.tensor.transpose(PS[4 + half + 2 * (t % 2)][:, (k % 4) * P:(k % 4 + 1) * P],
                                                      XN[:, t % 2, k * P:(k + 1) * P], IDENT)
                        ins.then_inc(ht_t, 1)
                    if t >= 1 and 3 + t < ADA:
                        ada(3 + t)

            @block.vector
            def _(dve):
                dve.wait_ge(lbi_in, 32)
                nc.vector.tensor_tensor(LBM[:], LBI[:, 0, :], LBI[:, 1, :], ALU.max).then_inc(lb_step, 1)
                dve.wait_ge(lb_step, 1)
                for j in range(2):
                    nc.vector.tensor_tensor(LBI[:, j, :], LBI[:, j, :], LBM[:], ALU.subtract) \
                      .then_inc(lb_step, 1)
                dve.wait_ge(cond_act, 3)
                nc.vector.tensor_tensor(CR[:], CR[:], CE[:], ALU.mult).then_inc(cond_silu, 1)
                dve.wait_ge(lb_exp, 1)
                nc.vector.tensor_tensor(LBS[:], LBI[:, 0, :], LBI[:, 1, :], ALU.add).then_inc(lb_step, 1)
                dve.wait_ge(lb_step, 4)
                nc.vector.reciprocal(LBM[:], LBS[:]).then_inc(lb_step, 1)
                dve.wait_ge(lb_step, 5)
                nc.vector.tensor_tensor(LBO[:, 0, :], LBI[:, 0, :], LBM[:], ALU.mult).then_inc(lb_step, 1)
                dve.wait_ge(lb_step, 6)
                nc.vector.tensor_scalar(LBO[:, 1, :], LBO[:, 0, :], -1.0, 1.0, ALU.mult, ALU.add) \
                  .then_inc(lb_step, 1)
                dve.wait_ge(cond_t, 1)
                nc.vector.tensor_copy(CT[:].rearrange("p k c -> p (k c)"), PS[0][:, 0:2 * KT]).then_inc(cond_ct, 1)
                nc.vector.tensor_copy(CW[:].rearrange("p k c -> p (k c)"), PS[0][:, 16:16 + 5 * KT])
                dve.wait_ge(rows_in, 48)

                def row(b):
                    dve.wait_ge(ada_mm, b + 1)
                    cols = slice(b * 512, (b + 1) * 512)
                    nc.vector.tensor_tensor(MODR[:, cols], MODR[:, cols], PS[1 + b % 2][0:2, :],
                                            ALU.add).then_inc(ada_row, 1)

                def fix(j, col, rows):
                    dve.wait_ge(ada_row, rows)
                    nc.vector.scalar_tensor_tensor(MODR[:, col:col + D], MODR[:, col:col + D], 1.0,
                                                   NR[:, j, :], ALU.add, ALU.mult).then_inc(mod_fix, 1)

                def normal(t):
                    dve.wait_ge(rs_done, t + 1)
                    if t >= 2:
                        dve.wait_ge(ht_t, 2 * (t - 1))
                    nc.vector.tensor_scalar(XN[:, t % 2], XT[:, t % 2], XR[:, t:t + 1], None,
                                            ALU.mult).then_inc(xn_done, 1)

                normal(0)
                normal(1)
                dve.wait_ge(ml_in, 16)
                nc.vector.tensor_copy(MLR[:], MLF[:]).then_inc(ml_made, 1)
                for b in range(4):
                    row(b)
                fix(0, D, 4)
                dve.wait_ge(mod_t, 1)
                nc.vector.tensor_copy(SH1T[:].rearrange("p k c -> p (k c)"), PS[3][:, 0:16])
                nc.vector.tensor_copy(A1T[:].rearrange("p k c -> p (k c)"), PS[3][:, 16:32]).then_inc(mod_ct, 1)
                for t in range(TN + 1):
                    if 2 <= t < TN:
                        normal(t)
                    if t > 0:
                        evac_h(dve, t - 1, 0)
                    if t > 1:
                        h_low(t - 2)
                    if t >= 2 and 2 + t < ADA:
                        row(2 + t)
                    if t == 7:
                        fix(1, 4 * D, ADA)
                    if t == TN - 1:
                        for slot in range(3):
                            dve.wait_ge(w_hi, slot + 1)
                            nc.vector.tensor_tensor(W[:, slot, 1], W_FULL[:, slot, 1],
                                                    W[:, slot, 0].bitcast(F32), ALU.subtract).then_inc(w_lo, 1)
                h_low(TN - 1)

            @block.gpsimd
            def _(pool):
                for t in range(2):
                    pool.dma_start(XT[:, t], x_rows[t]).then_inc(x_in_s[t], 16)
                pool.wait_ge(lb_step, 7)
                for d in range(2):
                    for j in range(2):
                        pool.dma_start(lb_d[j, d].rearrange("(c f) -> c f", f=P),
                                       LBO[8 * d:8 * d + 8, j, :]).then_inc(lb_out, 16)
                for t in range(2, TN):
                    pool.wait_ge(xn_done, t - 1)
                    pool.dma_start(XT[:, t % 2], x_rows[t]).then_inc(x_in_s[t % 2], 16)
                for i in range(3):
                    pool.wait_ge(ada_row, (6, 8, ADA)[i])
                    if i == 2:
                        pool.wait_ge(mod_fix, 2)
                    pool.dma_start(mod_d[:, i, :], MODR[:, (2 + i) * D:(3 + i) * D]).then_inc(mod_out, 16)

        next_stage()

        br = Region(nc, after_h, hi)
        QT = br("QT", [P, T])
        OGT = br("OGT", [P, T])
        LFL = nc.alloc_sbuf_tensor_at("LFL", [P, TN, 2, P], F32R, offset=br.at)
        LF = br("LF", [P, TN, 2, P])
        LFH = br("LFH", [P, TN, 2, P], F32R)
        KK = br("KK", [P, TN, 2, P])
        V = br("V", [P, TN, P])
        SS = br("SS", [P, 2, TL, P])
        SC = br("SC", [P, 2, P])
        LBB = br("LBB", [P, 2, 2, P])
        ZR = br("ZR", [P, 2, 2 * P])
        ZG = br("ZG", [P, 2, 2 * P])
        QR = br("QR", [P, 2, CH])
        KH = br("KH", [P, 2, 2, P])
        DEC = br("DEC", [P, 2, 2])
        EE = br("EE", [P, 2, 5, P])
        QE = br("QE", [P, 2, 2, 4, P])
        KE = br("KE", [P, 2, 3, P])
        SM = br("SM", [P, 2, P])
        SQJ = ZR[:, 0, 0:P]
        SSQ = br("SSQ", [P, 1])
        RST = br("RST", [P, 1])
        ON = br("ON", [P, P])
        OB = br("OB", [P, 2, P])
        CWP = br("CWP", [P, 5])
        CU = br("CU", [P, 2, CH])
        CC = br("CC", [P, 2, CH])
        CY = br("CY", [P, 2, CH])
        SGT = QR

        Z_STEPS = [("z", t) for t in range(TN)]
        QO_STEPS = [(kind, n) for kind in "qo" for n in range(NCH)]
        A_STEPS = [(kind, n) for n in range(NCH) for kind in "xcb"]
        G_STEPS = [(kind, n) for kind in "gh" for n in range(NCH)]
        STEPS = Z_STEPS + QO_STEPS + A_STEPS + G_STEPS
        NS = len(STEPS)
        assert NS % 2 == 0
        P1 = list(range(TL - 1)) + [CTX]
        N1 = len(P1)
        FILL1 = [2, 1, 1, 1, 1, 1, 1, 1]
        FILL2 = [2, 1, 1, 1, 1, 1, 1, 1, 3]
        assert len(FILL1) == N1 and sum(FILL1) + sum(FILL2) == NS - TN

        def fills(passes):
            j = TN if passes is FILL1 else TN + sum(FILL1)
            out = []
            for n in passes:
                out.append(list(range(j, j + n)))
                j += n
            return out

        head_done = {e: sem(f"head_done_{e}") for e in ("pe", "act", "dve", "pool", "sp")}
        product = sem("product")
        z_read = sem("z_read")
        z_ln = sem("z_ln")
        z_sig = sem("z_sig")
        z_gate = sem("z_gate")
        k_made = sem("k_made")
        f_made = sem("f_made")
        lf_made = sem("lf_made")
        lf_low = sem("lf_low")
        v_read = sem("v_read")
        qo_exp = sem("qo_exp")
        qo_ln = sem("qo_ln")
        qo_sig = sem("qo_sig")
        qo_read = sem("qo_read")
        x_read = sem("x_read")
        cg_read = sem("cg_read")
        tap1 = sem("tap1")
        conv_left = sem("conv_left")
        conv_done = sem("conv_done")
        bg_read = sem("bg_read")
        gate_read = sem("gate_read")
        gate_ln = sem("gate_ln")
        gate_sig = sem("gate_sig")
        tail_sum = sem("tail_sum")
        tail_read = sem("tail_read")
        khat = sem("khat")
        ds_done = sem("ds_done")
        state_upd = sem("state_upd")
        k_t = sem("k_t")
        e_sum = sem("e_sum")
        e_exp = sem("e_exp")
        qk_dec = sem("qk_dec")
        scores = sem("scores")
        masked = sem("masked")
        o_done = sem("o_done")
        o_sq = sem("o_sq")
        o_ln = sem("o_ln")
        o_rs = sem("o_rs")
        o_norm = sem("o_norm")
        o_t = sem("o_t")
        ob_made = sem("ob_made")
        cols_made = sem("cols_made")
        lb_in = sem("lb_in")
        st_in = sem("st_in")
        ya_out = [sem(f"ya_out{i}") for i in range(2)]
        ob_out = [sem(f"ob_out{i}") for i in range(2)]
        sg_out = [sem(f"sg_out{i}") for i in range(2)]
        sc_out = sem("sc_out")

        def tile_of(s, d):
            return s if s == CTX or d == 0 else TL - 1 - s

        w_oa_v, w_ob_v, w_o_v = (w[0].rearrange("(k p) n -> p k n", p=P) for w in (w_out_a, w_out_b, w_o))
        w_e_v = [w[0].rearrange("e (k p) n -> p e k n", p=P) for w in (w_ed, w_eg, w_eu)]

        def expert_weights(eng, slot, e):
            dst = WED[:, slot] if slot < 4 else WEA[:, slot - 4]
            eng.dma_start(dst, w_e_v[slot // 4][:, ds(e, 1), :, (slot % 4) * GW:(slot % 4 + 1) * GW]
                          .rearrange("p e k n -> p (e k) n")).then_inc(we_in[slot], 16)

        def step_no(step):
            return STEPS.index(step)

        def release(eng, g, j):
            kind = STEPS[j][0]
            kinds = {"q": "qo", "o": "qo", "g": "gh", "h": "gh"}.get(kind, kind)
            before = sum(1 for s in STEPS[:j + 1] if s[0] in kinds)
            s, per = {"z": (v_read, TN), "qo": (qo_read, 6), "x": (x_read, 3), "c": (cg_read, 3),
                      "b": (bg_read, 3), "gh": (gate_read, 6)}[kinds]
            eng.wait_ge(s, g * per + before)

        SPLITS = [3, 4, 0, 1, 2, 3, 4, 0, 1, 2]

        def split_of(kind):
            return {"q": 1, "o": 2, "x": 3, "c": 4, "b": 5, "g": 6, "h": 7}[kind] + 3

        def loads_of(slot, i):
            return {0: 1, 1: 1}.get(i, 2 if i < 7 else 3)

        with nc.Block() as block:
            @block.sync
            def _(sp):
                def head(g, last):
                    for e in ("pe", "dve"):
                        sp.wait_ge(head_done[e], g + 1)
                    for d in range(2):
                        sp.dma_start(SS[:, d, 0 if d == 0 else TL - 1],
                                     state[0, 0, d, ds(g, 1)].rearrange("a k v -> k (a v)")).then_inc(st_in, 16)
                    if not last:
                        sp.wait_ge(k_made, g * TN + TN)
                        sp.wait_ge(f_made, g * TN + TN)
                        bounds(g + 1)
                    for slot, (last_use, off) in enumerate(
                            ((("z", TN - 1), XI), (("z", TN - 1), CG), (("z", TN - 1), BG),
                             (("q", NCH - 1), GA), (("o", NCH - 1), GB))):
                        sp.wait_ge(product, g * NS + step_no(last_use) + 1)
                        wload(sp, slot, w_in_v, g * P + off)
                    def after(j):
                        kind, n = STEPS[j]
                        if kind == "b":
                            sp.wait_ge(bg_read, g * 3 + n + 1)
                            sp.dma_start(ya_d[ds(g * P, P), n * CH:(n + 1) * CH], CY[:, n % 2]) \
                              .then_inc(ya_out[n % 2], 16)
                        if kind in "gh":
                            i = n + (NCH if kind == "h" else 0)
                            sp.wait_ge(gate_sig, g * 6 + i + 1)
                            sp.dma_start(sg_d[i // NCH, ds(g * P, P), n * CH:(n + 1) * CH], SGT[:, i % 2]) \
                              .then_inc(sg_out[i % 2], 16)
                        if n == NCH - 1 and kind in "xcbgh":
                            slot = "xcbgh".index(kind)
                            sp.wait_ge(product, g * NS + j + 1)
                            if last:
                                wload(sp, slot, w_oa_v, slot * P)
                            else:
                                wload(sp, slot, w_in_v, (g + 1) * P + (ZF, ZB, IV, Q, OG)[slot])

                    for js in fills(FILL1):
                        for j in js:
                            if STEPS[j][0] not in "qo":
                                after(j)
                    sp.wait_ge(state_upd, g * N1 + N1)
                    for d in range(2):
                        sp.dma_start(new_state[0, 0, d, ds(g, 1)].rearrange("a k v -> k (a v)"),
                                     SC[:, d]).then_inc(sc_out, 16)
                    for t, js in enumerate(fills(FILL2)):
                        for j in js:
                            after(j)
                        if t >= 2:
                            ob_store(g, t - 2)
                    ob_store(g, TN - 2)
                    ob_store(g, TN - 1)
                    sp.wait_ge(sc_out, 32 * g + 32)
                    for i in range(2):
                        sp.wait_ge(ya_out[i], g * 16 * (2 - i) + 16 * (2 - i))
                        sp.wait_ge(ob_out[i], g * 16 * (5 - i) + 16 * (5 - i))
                        sp.wait_ge(sg_out[i], g * 48 + 48)
                        settled(sp)
                    sp.sem_inc(head_done["sp"], 1)

                def ob_store(g, t):
                    sp.wait_ge(ob_made, g * TN + t + 1)
                    sp.dma_start(ob_d[ds(g * P, P), t * P:(t + 1) * P], OB[:, t % 2]).then_inc(ob_out[t % 2], 16)

                def bounds(g):
                    for j in range(2):
                        for d in range(2):
                            sp.dma_start(LBB[:, j, d, :],
                                         lb_d[j, d, ds(g * P, P)].partition_broadcast(P)).then_inc(lb_in, 16)

                sp.sem_inc(head_done["sp"], 1)
                bounds(0)
                with sp.Fori(0, NH - 1) as g:
                    head(g, False)
                head(NH - 1, True)

            @block.tensor
            def _(pe):
                def product_step(g, j):
                    kind, at = STEPS[j]
                    if j >= 2:
                        release(pe, g, j - 2)
                    bank = PS[j % 2]
                    if at == 0:
                        pe.wait_ge(w_lo, g * 10 + (3 if kind == "z" else split_of(kind)))
                    slot = {"z": 0, "q": 3, "o": 4, "x": 0, "c": 1, "b": 2, "g": 3, "h": 4}[kind]
                    for i, (a, b) in enumerate(PARTS):
                        for k in range(KT):
                            if kind == "z":
                                lhs, rhs = HT[:, b, k, at * P:(at + 1) * P], W[:, 0:3, a, k, :]
                            else:
                                lhs, rhs = W[:, slot, a, k, :], HT[:, b, k, at * CH:(at + 1) * CH]
                            ins = nc.tensor.matmul(bank[:, 0:CH], lhs, rhs, start=(i == 0 and k == 0),
                                                   stop=(i == 2 and k == KT - 1))
                    ins.then_inc(product, 1)

                def tails(g, i):
                    s = P1[i]
                    if i == 0:
                        pe.wait_ge(lf_made, g * TN + TN)
                    if i >= 1:
                        pe.wait_ge(tail_read, g * N1 + i)
                    for d in range(2):
                        t = tile_of(s, d)
                        nc.tensor.matmul(PS[2 + i % 2][:, d * P:(d + 1) * P],
                                         CST[:, C_ST + d * P:C_ST + (d + 1) * P], LF[:, t, d, :],
                                         start=True, stop=True)
                    for d in range(2):
                        t = tile_of(s, d)
                        ins = nc.tensor.matmul(PS[4][:, d:d + 1], LF[:, t, d, :], ONE, start=True, stop=True)
                    ins.then_inc(tail_sum, 1)

                def contribution(g, i):
                    s = P1[i]
                    pe.wait_ge(khat, g * N1 + i + 1)
                    if i >= 2:
                        pe.wait_ge(state_upd, g * N1 + i - 1)
                    for d in range(2):
                        ins = nc.tensor.matmul(PS[5 + i % 2][:, d * P:(d + 1) * P], KH[:, i % 2, d, :],
                                               V[:, tile_of(s, d), :], start=True, stop=True)
                    ins.then_inc(ds_done, 1)

                def exponents(g, t, d):
                    if t:
                        pe.wait_ge(e_exp, g * 2 * TN + 2 * t + d - 1)
                    if d == 0:
                        pe.wait_ge(lf_low, g * TN + t + 1)
                    nc.tensor.matmul(PS[2 + d][:], LFH[:, t, d, :], MLR[:, d], start=True, stop=False)
                    nc.tensor.matmul(PS[2 + d][:], LFL[:, t, d, :], MLR[:, d], start=False, stop=True) \
                      .then_inc(e_sum, 1)

                def keys_t(g, t):
                    if t:
                        pe.wait_ge(qk_dec, g * 2 * TN + 2 * t)
                    for d in range(2):
                        ins = nc.tensor.transpose(PS[4][:, d * P:(d + 1) * P], KK[:, t, d, :], IDENT)
                    ins.then_inc(k_t, 1)

                def score(g, t, d):
                    pe.wait_ge(qk_dec, g * 2 * TN + 2 * t + d + 1)
                    if d == 0 and t:
                        pe.wait_ge(masked, g * TN + t)
                    q, k, out = QE[:, t % 2, d], KE[:, d], PS[5][:, d * P:(d + 1) * P]
                    nc.tensor.matmul(out, k[:, 0, :], q[:, 2, :], start=True, stop=True)
                    for j in range(2):
                        b = slice(64 * j, 64 * j + 64)
                        nc.tensor.matmul(out[b, b], k[:, 1, b], q[:, 3, b], start=True, stop=True)
                    for j in range(4):
                        b = slice(32 * j, 32 * j + 32)
                        ins = nc.tensor.matmul(out[b, b], k[:, 2, b], q[:, 1, b], start=True, stop=True)
                    ins.then_inc(scores, 1)

                def outputs(g, t):
                    pe.wait_ge(masked, g * TN + t + 1)
                    if t:
                        pe.wait_ge(o_norm, g * TN + t)
                    parts = []
                    for d in range(2):
                        if t != CTX:
                            parts.append((QE[:, t % 2, d, 0, :], SS[:, d, t, :]))
                        parts.append((SM[:, d, :], V[:, t, :]))
                    for i, (l, r) in enumerate(parts):
                        ins = nc.tensor.matmul(PS[6][:, 0:P], l, r, start=(i == 0), stop=(i == len(parts) - 1))
                    ins.then_inc(o_done, 1)

                def outputs_t(g, t):
                    pe.wait_ge(o_norm, g * TN + t + 1)
                    if t:
                        pe.wait_ge(ob_made, g * TN + t)
                    nc.tensor.transpose(PS[7][:, 0:P], ON[:], IDENT).then_inc(o_t, 1)

                pe.sem_inc(head_done["pe"], 1)
                with pe.Fori(0, NH) as g:
                    pe.wait_ge(head_done["act"], g + 1)
                    product_step(g, 0)
                    product_step(g, 1)
                    for e in ("dve", "pool"):
                        pe.wait_ge(head_done[e], g + 1)
                    for j in range(2, TN):
                        product_step(g, j)
                    for i, js in enumerate(fills(FILL1)):
                        if i == 0:
                            product_step(g, js.pop(0))
                        tails(g, i)
                        for j in js:
                            product_step(g, j)
                        contribution(g, i)
                    for t, js in enumerate(fills(FILL2)):
                        keys_t(g, t)
                        exponents(g, t, 0)
                        exponents(g, t, 1)
                        if t >= 2:
                            outputs_t(g, t - 2)
                        product_step(g, js[0])
                        if t:
                            outputs(g, t - 1)
                        score(g, t, 0)
                        score(g, t, 1)
                        if t < TN - 1:
                            for j in js[1:]:
                                product_step(g, j)
                        else:
                            product_step(g, js[1])
                            outputs_t(g, t - 1)
                    outputs(g, TN - 1)
                    product_step(g, js[2])
                    outputs_t(g, TN - 1)
                    pe.wait_ge(o_t, g * TN + TN)
                    pe.sem_inc(head_done["pe"], 1)

            @block.scalar
            def _(act):
                def high(g, i):
                    slot = SPLITS[i]
                    act.wait_ge(weights_in[slot], g * 32 + 16 * loads_of(slot, i))
                    nc.scalar.activation(W[:, slot, 0], W_FULL[:, slot, 1], ACT.Copy).then_inc(w_hi, 1)

                def sigmoid_z(g, t):
                    b = ZR[:, t % 2]
                    act.wait_ge(product, g * NS + step_no(("z", t)) + 1)
                    if t >= 2:
                        act.wait_ge(z_gate, g * TN + t - 1)
                    nc.scalar.activation(b, PS[step_no(("z", t)) % 2][:, 0:2 * P], ACT.Exp, scale=-1.0) \
                      .then_inc(z_read, 1)
                    act.wait_ge(z_read, g * TN + t + 1)
                    nc.scalar.activation(b, b, ACT.Ln, bias=1.0).then_inc(z_ln, 1)
                    if t:
                        log_f(g, t - 1)
                    act.wait_ge(z_ln, g * TN + t + 1)
                    nc.scalar.activation(b, b, ACT.Exp, scale=-1.0).then_inc(z_sig, 1)

                def log_f(g, t):
                    act.wait_ge(f_made, g * TN + t + 1)
                    nc.scalar.activation(LF[:, t].rearrange("p d n -> p (d n)"), ZG[:, t % 2], ACT.Ln)
                    nc.scalar.activation(LFH[:, t].rearrange("p d n -> p (d n)"), ZG[:, t % 2], ACT.Ln) \
                      .then_inc(lf_made, 1)

                def sigmoid_qo(g, j):
                    i = j - TN
                    b = QR[:, i % 2]
                    act.wait_ge(product, g * NS + j + 1)
                    if i < 2:
                        act.wait_ge(head_done["sp"], g + 1)
                    if i >= 2:
                        act.wait_ge(qo_read, g * 6 + i - 1)
                    nc.scalar.activation(b, PS[j % 2][:, 0:CH], ACT.Exp, scale=-1.0).then_inc(qo_exp, 1)
                    act.wait_ge(qo_exp, g * 6 + i + 1)
                    nc.scalar.activation(b, b, ACT.Ln, bias=1.0).then_inc(qo_ln, 1)
                    act.wait_ge(qo_ln, g * 6 + i + 1)
                    nc.scalar.activation(b, b, ACT.Exp, scale=-1.0).then_inc(qo_sig, 1)

                def sigmoid_gate(g, j):
                    i = j - step_no(("g", 0))
                    b = SGT[:, i % 2]
                    act.wait_ge(product, g * NS + j + 1)
                    if i >= 2:
                        act.wait_ge(sg_out[i % 2], g * 48 + 16 * (i // 2))
                    else:
                        act.wait_ge(qo_read, g * 6 + 6)
                    nc.scalar.activation(b, PS[j % 2][:, 0:CH], ACT.Exp, scale=-1.0).then_inc(gate_read, 1)
                    act.wait_ge(gate_read, g * 6 + i + 1)
                    nc.scalar.activation(b, b, ACT.Ln, bias=1.0).then_inc(gate_ln, 1)
                    act.wait_ge(gate_ln, g * 6 + i + 1)
                    nc.scalar.activation(b, b, ACT.Exp, scale=-1.0).then_inc(gate_sig, 1)

                def tail_exp(g, i):
                    act.wait_ge(tail_sum, g * N1 + i + 1)
                    if i >= 2:
                        act.wait_ge(ds_done, g * N1 + i - 1)
                        act.wait_ge(state_upd, g * N1 + i - 1)
                    nc.scalar.activation(KH[:, i % 2].rearrange("p d n -> p (d n)"), PS[2 + i % 2][:, 0:2 * P],
                                         ACT.Exp)
                    nc.scalar.activation(DEC[:, i % 2], PS[4][:, 0:2], ACT.Exp).then_inc(tail_read, 1)

                def level_exp(g, t, d):
                    e = EE[:, d]
                    n = g * 2 * TN + 2 * t + d
                    act.wait_ge(e_sum, n + 1)
                    if t:
                        act.wait_ge(qk_dec, n - 1)
                    nc.scalar.activation(e[:, 0:4, :], PS[2 + d][:], ACT.Exp)
                    nc.scalar.activation(e[:, 4, :], PS[2 + d][:, P:2 * P], ACT.Exp,
                                         scale=-1.0).then_inc(e_exp, 1)

                def conv_act(g, j):
                    kind, i = STEPS[j]
                    if kind == "x":
                        act.wait_ge(product, g * NS + j + 1)
                        if i >= 2:
                            act.wait_ge(conv_done, g * 3 + i - 1)
                        nc.scalar.activation(CU[:, i % 2], PS[j % 2][:, 0:CH], ACT.Copy).then_inc(x_read, 1)
                    elif kind == "c":
                        act.wait_ge(cols_made, g + 1)
                        act.wait_ge(cg_read, g * 3 + i + 1)
                        if i >= 2:
                            act.wait_ge(bg_read, g * 3 + i - 1)
                        nc.scalar.activation(CC[:, i % 2], CU[:, i % 2], ACT.Identity, bias=CWP[:, 3:4],
                                             scale=CWP[:, 1:2]).then_inc(tap1, 1)

                def o_rstd(g, t):
                    act.wait_ge(o_done, g * TN + t + 1)
                    if t:
                        act.wait_ge(o_rs, g * TN + t)
                    nc.scalar.activation(SQJ, PS[6][:, 0:P], ACT.Square, accum_out=SSQ[:]).then_inc(o_sq, 1)
                    act.wait_ge(o_sq, g * TN + t + 1)
                    nc.scalar.activation(SSQ[:], SSQ[:], ACT.Ln, bias=EPS, scale=1.0 / P).then_inc(o_ln, 1)
                    act.wait_ge(o_ln, g * TN + t + 1)
                    if t:
                        act.wait_ge(o_norm, g * TN + t)
                    nc.scalar.activation(RST[:], SSQ[:], ACT.Exp, scale=-0.5).then_inc(o_rs, 1)

                def filler(g, j):
                    kind = STEPS[j][0]
                    if kind in "qo":
                        sigmoid_qo(g, j)
                    elif kind in "gh":
                        sigmoid_gate(g, j)
                    else:
                        conv_act(g, j)

                act.sem_inc(head_done["act"], 1)
                with act.Fori(0, NH) as g:
                    for e in ("pe", "dve", "pool"):
                        act.wait_ge(head_done[e], g + 1)
                    for t in range(TN):
                        sigmoid_z(g, t)
                        for i in SPLIT_AT_Z.get(t, ()):
                            high(g, i)
                    log_f(g, TN - 1)
                    for s, js in enumerate(fills(FILL1)):
                        if s == 0:
                            filler(g, js.pop(0))
                        tail_exp(g, s)
                        for j in js:
                            filler(g, j)
                        for i in SPLIT_AT_1.get(s, ()):
                            high(g, i)
                    for t, js in enumerate(fills(FILL2)):
                        level_exp(g, t, 0)
                        level_exp(g, t, 1)
                        filler(g, js[0])
                        if t:
                            o_rstd(g, t - 1)
                        if t == TN - 1:
                            filler(g, js[1])
                            o_rstd(g, t)
                        for j in js[1 if t < TN - 1 else 2:]:
                            filler(g, j)
                        for i in SPLIT_AT_2.get(t, ()):
                            high(g, i)
                    act.wait_ge(o_rs, g * TN + TN)
                    act.sem_inc(head_done["act"], 1)

            @block.vector
            def _(dve):
                def low(g, i):
                    slot = SPLITS[i]
                    dve.wait_ge(w_hi, g * 10 + i + 4)
                    nc.vector.tensor_tensor(W[:, slot, 1], W_FULL[:, slot, 1],
                                            W[:, slot, 0].bitcast(F32), ALU.subtract).then_inc(w_lo, 1)

                def gate_z(g, t):
                    omlb = LBB[:, 1].rearrange("p d n -> p (d n)")
                    if t == 0:
                        dve.wait_ge(lb_in, g * 64 + 64)
                    dve.wait_ge(z_read, g * TN + t + 1)
                    nc.vector.tensor_copy(V[:, t], PS[step_no(("z", t)) % 2][:, 2 * P:3 * P]).then_inc(v_read, 1)
                    dve.wait_ge(z_sig, g * TN + t + 1)
                    if t >= 2:
                        dve.wait_ge(lf_made, g * TN + t - 1)
                        dve.wait_ge(k_made, g * TN + t - 1)
                    nc.vector.tensor_tensor(ZG[:, t % 2], ZR[:, t % 2], omlb, ALU.mult).then_inc(z_gate, 1)
                    dve.wait_ge(z_gate, g * TN + t + 1)
                    nc.vector.tensor_tensor(KK[:, t].rearrange("p d n -> p (d n)"), omlb, ZG[:, t % 2],
                                            ALU.subtract).then_inc(k_made, 1)

                def silu_qo(g, j):
                    i = j - TN
                    kind, n = STEPS[j]
                    src = PS[j % 2][:, 0:CH]
                    dve.wait_ge(qo_sig, g * 6 + i + 1)
                    if kind == "q":
                        ins = nc.vector.tensor_tensor(QT[:, n * CH:(n + 1) * CH], src, QR[:, i % 2], ALU.mult)
                    else:
                        ins = nc.vector.scalar_tensor_tensor(OGT[:, n * CH:(n + 1) * CH], src,
                                                             CWP[:, 4:5], QR[:, i % 2], ALU.mult, ALU.mult)
                    ins.then_inc(qo_read, 1)

                def log_f_low(g, t):
                    dve.wait_ge(tail_sum, g * N1 + N1)
                    nc.vector.tensor_tensor(LFL[:, t], LF[:, t], LFH[:, t].bitcast(F32),
                                            ALU.subtract).then_inc(lf_low, 1)

                def update(g, i):
                    s = P1[i]
                    dve.wait_ge(ds_done, g * N1 + i + 1)
                    if i == 0:
                        dve.wait_ge(st_in, g * 32 + 32)
                    else:
                        dve.wait_ge(state_upd, g * N1 + i)
                    src = PS[5 + i % 2]
                    if s == CTX:
                        dve.wait_ge(head_done["sp"], g + 1)
                        nc.vector.tensor_copy(SC[:].rearrange("p d v -> p (d v)"), src[:, 0:2 * P]) \
                          .then_inc(state_upd, 1)
                        return
                    for d in range(2):
                        here = tile_of(s, d)
                        there = here + (1 if d == 0 else -1)
                        ins = nc.vector.scalar_tensor_tensor(
                            SS[:, d, there, :], SS[:, d, here, :], DEC[:, i % 2, d:d + 1],
                            src[:, d * P:(d + 1) * P], ALU.mult, ALU.add)
                    ins.then_inc(state_upd, 1)

                def decayed(g, t, d):
                    n = g * 2 * TN + 2 * t + d
                    e = EE[:, d]
                    dve.wait_ge(e_exp, n + 1)
                    if d == 0:
                        dve.wait_ge(k_t, g * TN + t + 1)
                    if d == 0 and t >= 2:
                        dve.wait_ge(o_done, g * TN + t - 1)
                    if t:
                        dve.wait_ge(scores, n - 1)
                    q = QT[:, t * P:(t + 1) * P].unsqueeze(1).to_broadcast([P, 4, P])
                    nc.vector.tensor_tensor(QE[:, t % 2, d], q, e[:, 0:4, :], ALU.mult)
                    k = PS[4][:, d * P:(d + 1) * P].unsqueeze(1).to_broadcast([P, 3, P])
                    nc.vector.tensor_tensor(KE[:, d], k, e[:, 2:5, :], ALU.mult).then_inc(qk_dec, 1)

                def mask(g, t):
                    dve.wait_ge(scores, g * 2 * TN + 2 * t + 2)
                    if t:
                        dve.wait_ge(o_done, g * TN + t)
                    m = CST[:, C_MK:C_MK + 2 * P].rearrange("p (d n) -> p d n", d=2)
                    nc.vector.tensor_tensor(SM[:], PS[5][:, 0:2 * P].rearrange("p (d n) -> p d n", d=2), m,
                                            ALU.mult).then_inc(masked, 1)

                def normed(g, t):
                    dve.wait_ge(o_rs, g * TN + t + 1)
                    if t:
                        dve.wait_ge(o_t, g * TN + t)
                    nc.vector.tensor_scalar(ON[:], PS[6][:, 0:P], RST[:], None, ALU.mult).then_inc(o_norm, 1)

                def gated(g, t):
                    dve.wait_ge(o_t, g * TN + t + 1)
                    if t >= 2:
                        dve.wait_ge(ob_out[t % 2], g * 16 * (5 - t % 2) + 16 * (t // 2))
                    else:
                        dve.wait_ge(head_done["sp"], g + 1)
                    nc.vector.tensor_tensor(OB[:, t % 2], PS[7][:, 0:P], OGT[:, t * P:(t + 1) * P],
                                            ALU.mult).then_inc(ob_made, 1)

                def conv_dve(g, j):
                    kind, i = STEPS[j]
                    u, c, y = CU[:, i % 2], CC[:, i % 2], CY[:, i % 2]
                    tap = [CWP[:, k:k + 1] for k in range(3)]
                    if kind == "c":
                        dve.wait_ge(product, g * NS + j + 1)
                        dve.wait_ge(x_read, g * 3 + i + 1)
                        nc.vector.tensor_tensor(u, u, PS[j % 2][:, 0:CH], ALU.mult).then_inc(cg_read, 1)
                    if kind == "b":
                        cuts = [(0, CH, ROW)] if i < NCH - 1 else [(0, CH - P, ROW), (CH - P, CH, P)]
                        dve.wait_ge(tap1, g * 3 + i + 1)
                        for lo_, hi_, row in cuts:
                            cv = c[:, lo_:hi_].rearrange("p (r w) -> p r w", w=row)
                            uv = u[:, lo_:hi_].rearrange("p (r w) -> p r w", w=row)
                            ins = nc.vector.scalar_tensor_tensor(cv[:, :, 1:], uv[:, :, :row - 1], tap[0],
                                                                 cv[:, :, 1:], ALU.mult, ALU.add)
                        ins.then_inc(conv_left, 1)
                        dve.wait_ge(conv_left, g * 3 + i + 1)
                        for lo_, hi_, row in cuts:
                            cv = c[:, lo_:hi_].rearrange("p (r w) -> p r w", w=row)
                            uv = u[:, lo_:hi_].rearrange("p (r w) -> p r w", w=row)
                            ins = nc.vector.scalar_tensor_tensor(cv[:, :, :row - 1], uv[:, :, 1:], tap[2],
                                                                 cv[:, :, :row - 1], ALU.mult, ALU.add)
                        ins.then_inc(conv_done, 1)
                        dve.wait_ge(conv_done, g * 3 + i + 1)
                        dve.wait_ge(product, g * NS + j + 1)
                        if i >= 2:
                            dve.wait_ge(ya_out[0], g * 32 + 16)
                        else:
                            dve.wait_ge(head_done["sp"], g + 1)
                        nc.vector.tensor_tensor(y, c, PS[j % 2][:, 0:CH], ALU.mult).then_inc(bg_read, 1)

                def filler(g, j):
                    kind = STEPS[j][0]
                    if kind in "qo":
                        silu_qo(g, j)
                    elif kind in "xcb":
                        conv_dve(g, j)

                dve.sem_inc(head_done["dve"], 1)
                with dve.Fori(0, NH) as g:
                    for e in ("pe", "act", "pool"):
                        dve.wait_ge(head_done[e], g + 1)
                    nc.vector.tensor_scalar(CWP[:].unsqueeze(1), CW[:, ds(g, 1), :], 1.0, None, ALU.mult) \
                      .then_inc(cols_made, 1)
                    dve.wait_ge(cols_made, g + 1)
                    for t in range(TN):
                        gate_z(g, t)
                        for i in SPLIT_AT_Z.get(t, ()):
                            low(g, i)
                    for s, js in enumerate(fills(FILL1)):
                        if s == N1 - 1:
                            log_f_low(g, 0)
                        for j in js:
                            filler(g, j)
                        update(g, s)
                        for i in SPLIT_AT_1.get(s, ()):
                            low(g, i)
                    for t, js in enumerate(fills(FILL2)):
                        if t < TN - 1:
                            log_f_low(g, t + 1)
                        decayed(g, t, 0)
                        if t >= 2:
                            gated(g, t - 2)
                        decayed(g, t, 1)
                        filler(g, js[0])
                        if t:
                            normed(g, t - 1)
                        mask(g, t)
                        for j in js[1:]:
                            filler(g, j)
                        for i in SPLIT_AT_2.get(t, ()):
                            low(g, i)
                    gated(g, TN - 2)
                    normed(g, TN - 1)
                    gated(g, TN - 1)
                    dve.wait_ge(ob_made, g * TN + TN)
                    dve.sem_inc(head_done["dve"], 1)

            @block.gpsimd
            def _(pool):
                def forget(g, t):
                    if t == 0:
                        pool.wait_ge(lb_in, g * 64 + 64)
                    pool.wait_ge(k_made, g * TN + t + 1)
                    nc.gpsimd.tensor_tensor(ZG[:, t % 2], ZG[:, t % 2], LBB[:, 0].rearrange("p d n -> p (d n)"),
                                            ALU.add).then_inc(f_made, 1)

                def key_hat(g, i):
                    s = P1[i]
                    pool.wait_ge(tail_read, g * N1 + i + 1)
                    for d in range(2):
                        ins = nc.gpsimd.tensor_tensor(KH[:, i % 2, d], KH[:, i % 2, d],
                                                      KK[:, tile_of(s, d), d, :], ALU.mult)
                    ins.then_inc(khat, 1)

                pool.sem_inc(head_done["pool"], 1)
                with pool.Fori(0, NH) as g:
                    for e in ("pe", "act", "dve"):
                        pool.wait_ge(head_done[e], g + 1)
                    for t in range(TN):
                        forget(g, t)
                    for i in range(N1):
                        key_hat(g, i)
                    pool.wait_ge(khat, g * N1 + N1)
                    pool.sem_inc(head_done["pool"], 1)

        if upto == "branches":
            return

        next_stage()

        MIX = nc.alloc_sbuf_tensor_at("MIX", [P, KT, T], F32, offset=hi - KT * T * 4)
        YO = nc.alloc_sbuf_tensor_at("YO", [P, 2, KT, T], F32R, offset=HT_OFF)
        mg = Region(nc, after_h, hi - KT * T * 4)
        YO_FULL = nc.alloc_sbuf_tensor_at("YO_FULL", [P, 2, KT, T], F32, offset=HT_OFF)
        OBL_FULL = nc.alloc_sbuf_tensor_at("OBL_FULL", [P, KT, T], F32, offset=mg.at)
        OBL = mg("OBL", [P, KT, T], F32R)
        GL = mg("GL", [P, 4, CH])
        MP = mg("MP", [P, 2, CH])
        NB = 2 * KT
        ch_in = [sem(f"ch_in{i}") for i in range(2 * NCH)]
        ch_hi = sem("ch_hi")
        ch_lo = sem("ch_lo")
        sg_in = [sem(f"sg_in{i}") for i in range(4)]
        sg_used = sem("sg_used")
        m_product = sem("m_product")
        m_part = sem("m_part")
        m_a = sem("m_a")
        m_sum = sem("m_sum")

        with nc.Block() as block:
            @block.sync
            def _(sp):
                for p, (dst, src) in enumerate(((YO_FULL[:, 1], ya_d), (OBL_FULL[:], ob_d))):
                    for n in range(NCH):
                        cols = slice(n * CH, (n + 1) * CH)
                        sp.dma_start(dst[:, :, cols],
                                     src.rearrange("(k p) t -> p k t", p=P)[:, :, cols]) \
                          .then_inc(ch_in[p * NCH + n], 16)
                for b in range(4, NB):
                    sp.wait_ge(m_product, (b - 3) * NCH)
                    wload(sp, b % 4, w_oa_v if b < KT else w_ob_v, (b % KT) * P)
                    if b == KT + 3:
                        for slot in range(4):
                            sp.dma_start(WED[:, slot], w_o_v[:, :, slot * GW:(slot + 1) * GW]).then_inc(wo_in, 16)

            @block.gpsimd
            def _(pool):
                with pool.Fori(0, NB // 4) as s:
                    for j in range(4 * NCH):
                        m, n = j // NCH, j % NCH
                        pool.wait_ge(sg_used, s * 4 * NCH + j + 1)
                        settled(pool)
                        pool.dma_start(GL[:, j % 4], sg_flat[ds(s * 4 * P + m * P, P), n * CH:(n + 1) * CH]) \
                            .then_inc(sg_in[j % 4], 16)

            @block.tensor
            def _(pe):
                for p in range(2):
                    with pe.Fori(0, 2) as s:
                        for m in range(4):
                            for n in range(NCH):
                                j = m * NCH + n
                                step = s * 4 * NCH + (p * KT * NCH + j)
                                if n == 0:
                                    pe.wait_ge(w_lo, s * 4 + (W_SPLIT + p * KT + m + 1))
                                if m == 0:
                                    pe.wait_ge(ch_hi, p * NCH + n + 1)
                                pe.wait_ge(sg_used, step + 1)
                                for i, (a, b) in enumerate(PARTS):
                                    src = OBL[:] if (p, b) == (1, 1) else YO[:, b]
                                    if m == 0 and b == 1:
                                        pe.wait_ge(ch_lo, p * NCH + n + 1)
                                    for k in range(KT):
                                        ins = nc.tensor.matmul(PS[j % 4][:, 0:CH], W[:, m, a, k, :],
                                                               src[:, k, n * CH:(n + 1) * CH],
                                                               start=(i == 0 and k == 0),
                                                               stop=(i == 2 and k == KT - 1))
                                ins.then_inc(m_product, 1)

            @block.scalar
            def _(act):
                def chunk(i):
                    cols = slice(i % NCH * CH, (i % NCH + 1) * CH)
                    src = YO_FULL[:, 1] if i < NCH else OBL_FULL[:]
                    act.wait_ge(ch_in[i], 16)
                    if i >= NCH:
                        act.wait_ge(m_product, (KT - 1) * NCH + (i - NCH) + 1)
                    nc.scalar.activation(YO[:, 0, :, cols], src[:, :, cols], ACT.Copy).then_inc(ch_hi, 1)

                for i in range(NCH):
                    chunk(i)
                for b in range(3, NB):
                    act.wait_ge(weights_in[b % 4], 16 * (2 * NH + 1 + b // 4))
                    nc.scalar.activation(W[:, b % 4, 0], W_FULL[:, b % 4, 1], ACT.Copy).then_inc(w_hi, 1)
                    if b == KT + 2:
                        for i in range(NCH, 2 * NCH):
                            chunk(i)

            @block.vector
            def _(dve):
                def chunk(i):
                    cols = slice(i % NCH * CH, (i % NCH + 1) * CH)
                    if i < NCH:
                        dst, full = YO[:, 1, :, cols], YO_FULL[:, 1, :, cols]
                    else:
                        dst, full = OBL[:, :, cols], OBL_FULL[:, :, cols]
                    dve.wait_ge(ch_hi, i + 1)
                    nc.vector.tensor_tensor(dst, full, YO[:, 0, :, cols].bitcast(F32),
                                            ALU.subtract).then_inc(ch_lo, 1)

                def gate(s, p, m, n):
                    j = m * NCH + n
                    step = s * 4 * NCH + (p * KT * NCH + j)
                    out = MIX[:, ds(4 * s + m, 1), n * CH:(n + 1) * CH]
                    dve.wait_ge(m_product, step + 1)
                    dve.wait_ge(sg_in[j % 4], s * 48 + (p * 96 + 16 * (j // 4) + 16))
                    if p == 0:
                        ins = nc.vector.tensor_tensor(out, PS[j % 4][:, 0:CH].unsqueeze(1),
                                                      GL[:, j % 4].unsqueeze(1), ALU.mult)
                        ins.then_inc(sg_used, 1)
                    else:
                        part = MP[:, j % 2]
                        nc.vector.tensor_tensor(part, PS[j % 4][:, 0:CH], GL[:, j % 4], ALU.mult) \
                          .then_inc(sg_used, 1)
                        dve.wait_ge(sg_used, step + 5)
                        nc.vector.tensor_tensor(out, out, part.unsqueeze(1), ALU.add).then_inc(m_sum, 1)

                def low(s, b):
                    dve.wait_ge(w_hi, s * 4 + (W_SPLIT + b + 1))
                    nc.vector.tensor_tensor(W[:, b % 4, 1], W_FULL[:, b % 4, 1],
                                            W[:, b % 4, 0].bitcast(F32), ALU.subtract).then_inc(w_lo, 1)

                dve.sem_inc(sg_used, 4)
                for i in range(NCH):
                    chunk(i)
                with dve.Fori(0, 2) as s:
                    for m in range(4):
                        low(s, m + 3)
                        for n in range(NCH):
                            gate(s, 0, m, n)
                for i in range(NCH, 2 * NCH):
                    chunk(i)
                dve.wait_ge(sg_used, 4 + KT * NCH)
                for s in range(2):
                    for m in range(4):
                        if KT + 4 * s + m + 3 < NB:
                            low(s, KT + m + 3)
                        for n in range(NCH):
                            gate(s, 1, m, n)

        next_stage()

        mx = Region(nc, W_OFF + 8 * SLOT, WED_OFF)
        TA = mx("TA", [P, TN, NE + 1, 2])
        POST = mx("POST", [P, TN, NE + 1])
        H2T = mx("H2T", [P, KT, P])
        AFT = mx("AFT", [NE, T])
        WR = mx("WR", [P, KT, NE])
        WOH = nc.alloc_sbuf_tensor_at("WOH", [P, 4, KT, GW], F32R, offset=W_OFF + 4 * SLOT)
        WOL = nc.alloc_sbuf_tensor_at("WOL", [P, 4, KT, GW], F32R, offset=WED_OFF)
        MIXL = nc.alloc_sbuf_tensor_at("MIXL", [P, KT, T], F32R, offset=hi - KT * T * 4)
        after_w = WED_OFF + 4 * SLOT
        mx = Region(nc, after_w, hi - KT * T * 4)
        G1 = mx("G1", [P, 2, D])
        SH2 = mx("SH2", [P, 2, D])
        A2 = mx("A2", [P, 2, D])
        XL = mx("XL", [P, 2, D])
        X1 = mx("X1", [P, 2, D])
        H2 = mx("H2", [P, 2, D])
        MH_FULL = nc.alloc_sbuf_tensor_at("MH_FULL", [P, 2, D], F32, offset=mx.at)
        MH = mx("MH", [P, 2, KT, P], F32R)
        RS2 = mx("RS2", [P, 2, TN])
        SMX = mx("SMX", [P, 3, TN])
        LEX = mx("LEX", [P, 2, NE])
        sl = Region(nc, hi - KT * T * 4, hi)
        WK = sl("WK", [NE, T])
        SEL = sl("SEL", [NE, T])
        CUM = sl("CUM", [NE, T])
        M8 = sl("M8", [NE, 2, 8])
        AWG = sl("AWG", [P, KT, 512])
        MG = sl("MG", [2, D])

        modv_in = sem("modv_in")
        bg2_in = sem("bg2_in")
        awg_in = sem("awg_in")
        g2_mm = sem("g2_mm")
        g2_row = sem("g2_row")
        wr_in = sem("wr_in")
        xl_in = [sem(f"xl_in{i}") for i in range(2)]
        wo_hi = sem("wo_hi")
        wo_lo = sem("wo_lo")
        mix_hi = sem("mix_hi")
        mix_lo = sem("mix_lo")
        mix_mm = sem("mix_mm")
        x1_g = sem("x1_g")
        x1_made = sem("x1_made")
        x1_out = [sem(f"x1_out{i}") for i in range(2)]
        n2_sq = sem("n2_sq")
        n2_ln = sem("n2_ln")
        n2_rs = sem("n2_rs")
        h2_a = sem("h2_a")
        h2_made = sem("h2_made")
        h2_out = [sem(f"h2_out{i}") for i in range(2)]
        h2_t = sem("h2_t")
        h2_sb = sem("h2_sb")
        logits = sem("logits")
        lg_max = sem("lg_max")
        lg_exp = sem("lg_exp")
        lg_rec = sem("lg_rec")
        aff_made = sem("aff_made")
        aff_t = sem("aff_t")
        aft_made = sem("aft_made")
        topk = sem("topk")
        ta_init = sem("ta_init")
        pos_made = sem("pos_made")
        pos_t = sem("pos_t")
        post_made = sem("post_made")
        ORDER = list(range(TN))

        with nc.Block() as block:
            @block.sync
            def _(sp):
                for i, dst in enumerate((G1, SH2, A2)):
                    for c in range(2):
                        sp.dma_start(dst[:, c], mod_d[c, i].partition_broadcast(P)).then_inc(modv_in, 16)
                sp.dma_start(WR[:], w_router[0].rearrange("(k p) e -> p k e", p=P)).then_inc(wr_in, 16)
                for i, t in enumerate(ORDER):
                    if i >= 2:
                        sp.wait_ge(x1_made, i - 1)
                    sp.dma_start(XL[:, i % 2], x_rows[t]).then_inc(xl_in[i % 2], 16)
                for slot in range(4, 8):
                    expert_weights(sp, slot, 0)
                sp.wait_ge(mix_mm, 2 * TN)
                sp.dma_start(MG[:], b_ada[0, 5 * D:6 * D].partition_broadcast(2)).then_inc(bg2_in, 16)
                for i, slot in enumerate((8, 9, 10, 11, 0, 1, 2, 3)):
                    if i in (0, 2):
                        b = ADA + i // 2
                        if i:
                            sp.wait_ge(g2_mm, 1)
                        sp.dma_start(AWG[:], w_ada_v[:, :, b * 512:(b + 1) * 512]).then_inc(awg_in, 16)
                    expert_weights(sp, slot, 0)

            @block.gpsimd
            def _(pool):
                nc.gpsimd.memset(TA[:], 0.0).then_inc(ta_init, 1)
                nc.gpsimd.memset(POST[:], 0.0).then_inc(ta_init, 1)
                pool.wait_ge(ta_init, 2)
                for t in range(TN):
                    ins = nc.gpsimd.tensor_copy(TA[:, t, 0:NE, 0], CST[:, C_TOK + t:C_TOK + t + 1]
                                                .to_broadcast([P, NE]))
                ins.then_inc(ta_init, 1)
                for i, t in enumerate(ORDER):
                    c = 0 if t == CTX else 1
                    pool.wait_ge(x1_g, 2 * i + 2)
                    pool.wait_ge(xl_in[i % 2], 16 * (i // 2 + 1))
                    nc.gpsimd.tensor_tensor(X1[:, i % 2], X1[:, i % 2], XL[:, i % 2], ALU.add) \
                      .then_inc(x1_made, 1)
                    pool.wait_ge(x1_made, i + 1)
                    pool.dma_start(x1_d[t * P:(t + 1) * P, :], X1[:, i % 2]).then_inc(x1_out[i % 2], 16)
                    pool.wait_ge(h2_a, i + 1)
                    nc.gpsimd.tensor_tensor(H2[:, i % 2], H2[:, i % 2], SH2[:, c], ALU.add).then_inc(h2_made, 1)
                    pool.wait_ge(h2_made, i + 1)
                    pool.dma_start(h2_d[t * P:(t + 1) * P, :], H2[:, i % 2]).then_inc(h2_out[i % 2], 16)
                for s in (x1_out, h2_out):
                    pool.wait_ge(s[0], 80)
                    pool.wait_ge(s[1], 64)

            @block.tensor
            def _(pe):
                def mix_half(i, h):
                    t = ORDER[i]
                    if h == 0:
                        pe.wait_ge(mix_hi, i + 1)
                    if i == 0:
                        pe.wait_ge(wo_hi, 2 * h + 2)
                    if i >= 2:
                        pe.wait_ge(x1_g, 2 * (i - 2) + h + 1)
                    for j, (a, b) in enumerate(PARTS):
                        if i == 0 and a == 1:
                            pe.wait_ge(wo_lo, 2 * h + 2)
                        if h == 0 and b == 1:
                            pe.wait_ge(mix_lo, i + 1)
                        for k in range(KT):
                            lhs = MIXL[:, k, t * P:(t + 1) * P] if b else MH[:, i % 2, k, :]
                            ins = nc.tensor.matmul(PS[2 * (i % 2) + h][:], lhs,
                                                   (WOH, WOL)[a][:, 2 * h:2 * h + 2, k, :],
                                                   start=(j == 0 and k == 0), stop=(j == 2 and k == KT - 1))
                    ins.then_inc(mix_mm, 1)

                def rows_t(i):
                    pe.wait_ge(h2_made, i + 1)
                    if i:
                        pe.wait_ge(h2_sb, 2 * i)
                    for h in range(2):
                        for k in range(4 * h, 4 * h + 4):
                            ins = nc.tensor.transpose(PS[4 + h][:, (k % 4) * P:(k % 4 + 1) * P],
                                                      H2[:, i % 2, k * P:(k + 1) * P], IDENT)
                        ins.then_inc(h2_t, 1)

                def router(i):
                    pe.wait_ge(h2_sb, 2 * i + 2)
                    if i:
                        pe.wait_ge(lg_exp, i)
                    else:
                        pe.wait_ge(wr_in, 16)
                    for k in range(KT):
                        ins = nc.tensor.matmul(PS[6][:, 0:NE], H2T[:, k, :], WR[:, k, :], start=(k == 0),
                                               stop=(k == KT - 1))
                    ins.then_inc(logits, 1)

                def affinity_t(i):
                    t = ORDER[i]
                    pe.wait_ge(aff_made, i + 1)
                    if i:
                        pe.wait_ge(aft_made, i)
                    nc.tensor.transpose(PS[7][0:NE, 0:P], TA[:, t, 0:NE, 1], IDENT).then_inc(aff_t, 1)

                for i in range(TN + 2):
                    if i < TN:
                        mix_half(i, 0)
                    if i >= 2:
                        router(i - 2)
                    if i < TN:
                        mix_half(i, 1)
                    if 1 <= i <= TN:
                        rows_t(i - 1)
                    if 2 <= i <= TN:
                        affinity_t(i - 2)
                pe.wait_ge(x1_g, 2 * TN)
                for i in range(2):
                    pe.wait_ge(awg_in, 16 * i + 16)
                    for k in range(KT):
                        ins = nc.tensor.matmul(PS[1 + i][0:2, :], CT[:, k, :], AWG[:, k, :],
                                               start=(k == 0), stop=(k == KT - 1))
                    ins.then_inc(g2_mm, 1)
                affinity_t(TN - 1)
                pe.wait_ge(pos_made, 1)
                for t in range(TN):
                    ins = nc.tensor.transpose(PS[0][:, t * NE:(t + 1) * NE], CUM[:, t * P:(t + 1) * P],
                                              IDENT[0:NE, 0:NE])
                ins.then_inc(pos_t, 1)

            @block.scalar
            def _(act):
                def mix_high(i):
                    t = ORDER[i]
                    if i >= 2:
                        act.wait_ge(n2_sq, i - 1)
                    nc.scalar.activation(MH[:, i % 2], MIX[:, :, t * P:(t + 1) * P], ACT.Copy).then_inc(mix_hi, 1)

                act.wait_ge(wo_in, 64)
                mix_high(0)
                for slot in range(4):
                    nc.scalar.activation(WOH[:, slot], WED[:, slot], ACT.Copy).then_inc(wo_hi, 1)
                mix_high(1)
                for i in range(TN + 1):
                    if i < TN:
                        t = ORDER[i]
                        act.wait_ge(x1_made, i + 1)
                        if i:
                            act.wait_ge(n2_sq, i)
                        nc.scalar.activation(MH_FULL[:, i % 2], X1[:, i % 2], ACT.Square,
                                             accum_out=RS2[:, 0, i:i + 1]).then_inc(n2_sq, 1)
                        act.wait_ge(n2_sq, i + 1)
                        nc.scalar.activation(RS2[:, 0, i:i + 1], RS2[:, 0, i:i + 1], ACT.Ln, bias=EPS,
                                             scale=1.0 / D).then_inc(n2_ln, 1)
                        act.wait_ge(n2_ln, i + 1)
                        nc.scalar.activation(RS2[:, 1, i:i + 1], RS2[:, 0, i:i + 1], ACT.Exp,
                                             scale=-0.5).then_inc(n2_rs, 1)
                        if i + 2 < TN:
                            mix_high(i + 2)
                    if i >= 1:
                        act.wait_ge(lg_max, i)
                        if i >= 3:
                            act.wait_ge(aff_made, i - 2)
                        nc.scalar.activation(LEX[:, (i - 1) % 2], PS[6][:, 0:NE], ACT.Exp,
                                             bias=SMX[:, 0, i - 1:i], accum_out=SMX[:, 1, i - 1:i]) \
                          .then_inc(lg_exp, 1)
                    if i < TN:
                        if i:
                            act.wait_ge(logits, i)
                        for h in range(2):
                            act.wait_ge(h2_t, 2 * i + h + 1)
                            nc.scalar.activation(H2T[:, 4 * h:4 * h + 4, :].rearrange("p k n -> p (k n)"),
                                                 PS[4 + h][:], ACT.Copy).then_inc(h2_sb, 1)

            @block.vector
            def _(dve):
                def mix_low(i):
                    t = ORDER[i]
                    dve.wait_ge(mix_hi, i + 1)
                    cols = slice(t * P, (t + 1) * P)
                    nc.vector.tensor_tensor(MIXL[:, :, cols], MIX[:, :, cols], MH[:, i % 2].bitcast(F32),
                                            ALU.subtract).then_inc(mix_lo, 1)

                def residual(i):
                    c = 0 if ORDER[i] == CTX else 1
                    if i == 0:
                        dve.wait_ge(modv_in, 96)
                    for h in range(2):
                        dve.wait_ge(mix_mm, 2 * i + h + 1)
                        if i >= 2 and h == 0:
                            dve.wait_ge(x1_out[i % 2], 16 * (i // 2))
                            dve.wait_ge(n2_sq, i - 1)
                        cols = slice(512 * h, 512 * h + 512)
                        nc.vector.tensor_tensor(X1[:, i % 2, cols], PS[2 * (i % 2) + h][:], G1[:, c, cols],
                                                ALU.mult).then_inc(x1_g, 1)

                def scaled(i):
                    c = 0 if ORDER[i] == CTX else 1
                    dve.wait_ge(n2_rs, i + 1)
                    if i >= 2:
                        dve.wait_ge(h2_out[i % 2], 16 * (i // 2))
                        dve.wait_ge(h2_t, 2 * (i - 1))
                    nc.vector.scalar_tensor_tensor(H2[:, i % 2], X1[:, i % 2], RS2[:, 1, i:i + 1], A2[:, c],
                                                   ALU.mult, ALU.mult).then_inc(h2_a, 1)

                def softmax_max(i):
                    dve.wait_ge(logits, i + 1)
                    nc.vector.tensor_reduce(SMX[:, 0, i:i + 1], PS[6][:, 0:NE], AX.X, ALU.max,
                                            negate=True).then_inc(lg_max, 1)

                def softmax_end(i):
                    dve.wait_ge(lg_exp, i + 1)
                    nc.vector.reciprocal(SMX[:, 2, i:i + 1], SMX[:, 1, i:i + 1]).then_inc(lg_rec, 1)
                    dve.wait_ge(lg_rec, i + 1)
                    if i == 0:
                        dve.wait_ge(ta_init, 3)
                    nc.vector.tensor_scalar(TA[:, ORDER[i], 0:NE, 1], LEX[:, i % 2], SMX[:, 2, i:i + 1], None,
                                            ALU.mult).then_inc(aff_made, 1)

                def affinity_rows(i):
                    t = ORDER[i]
                    dve.wait_ge(aff_t, i + 1)
                    nc.vector.tensor_copy(AFT[:, t * P:(t + 1) * P], PS[7][0:NE, 0:P]).then_inc(aft_made, 1)

                n = [0]

                def chained(ins):
                    ins.then_inc(topk, 1)
                    n[0] += 1
                    dve.wait_ge(topk, n[0])

                def select(lo_, hi_, cap):
                    chained(nc.vector.tensor_copy(WK[:, lo_:hi_], AFT[:, lo_:hi_]))
                    for r in range(cap // 8):
                        chained(nc.vector.max(M8[:, r % 2], WK[:, lo_:hi_]))
                        chained(nc.vector.match_replace(WK[:, lo_:hi_], M8[:, r % 2], WK[:, lo_:hi_], -1.0))
                    chained(nc.vector.tensor_scalar(SEL[:, lo_:hi_], WK[:, lo_:hi_], 0.0, None, ALU.is_lt))
                    chained(nc.vector.tensor_tensor_scan(CUM[:, lo_:hi_], SEL[:, lo_:hi_], SEL[:, lo_:hi_],
                                                         0.0, ALU.add, ALU.max))

                for slot in range(4):
                    dve.wait_ge(wo_hi, slot + 1)
                    nc.vector.tensor_tensor(WOL[:, slot], WED[:, slot], WOH[:, slot].bitcast(F32),
                                            ALU.subtract).then_inc(wo_lo, 1)
                    if slot == 1:
                        mix_low(0)
                mix_low(1)
                for i in range(TN):
                    residual(i)
                    if i + 2 < TN:
                        mix_low(i + 2)
                    scaled(i)
                    if i:
                        softmax_max(i - 1)
                        softmax_end(i - 1)
                    if i >= 2:
                        affinity_rows(i - 2)
                affinity_rows(TL - 1)
                dve.wait_ge(aft_made, TL)
                dve.wait_ge(mix_mm, 2 * TN)
                select(0, TL * P, CAP_L)
                softmax_max(TN - 1)
                softmax_end(TN - 1)
                affinity_rows(TN - 1)
                dve.wait_ge(aft_made, TN)
                select(TL * P, T, CAP_C)
                dve.wait_ge(bg2_in, 16)
                for i in range(2):
                    dve.wait_ge(g2_mm, i + 1)
                    cols = slice(i * 512, (i + 1) * 512)
                    nc.vector.tensor_tensor(MG[:, cols], MG[:, cols], PS[1 + i][0:2, :],
                                            ALU.add).then_inc(g2_row, 1)
                nc.vector.tensor_tensor(CUM[:], CUM[:], SEL[:], ALU.mult).then_inc(pos_made, 1)
                dve.wait_ge(pos_t, 1)
                nc.vector.tensor_copy(POST[:, :, 0:NE], PS[0][:, 0:TN * NE].rearrange("p (t e) -> p t e", t=TN)) \
                  .then_inc(post_made, 1)

        if upto == "mixing":
            return

        next_stage()

        NX = CAP_L + CAP_C
        ex = Region(nc, after_w, hi)
        G2 = ex("G2", [P, 2, D])
        OH = ex("OH", [P, TN, P])
        IDX = ex("IDX", [P, 2, 2], U32)
        TW = ex("TW", [P, 2, 2])
        XG = ex("XG", [P, D])
        XC = ex("XC", [CAP_C, D])
        XET = ex("XET", [P, KT, NX])
        SG = ex("SG", [P, 2, NX])
        GU = ex("GU", [P, 2, NX])
        HID = ex("HID", [P, KT, NX])
        YT = ex("YT", [P, 2, 4, NX])
        YS = ex("YS", [P, D])
        YC = ex("YC", [CAP_C, D])

        g2_out = sem("g2_out")
        g2_in = sem("g2_in")
        oh_made = sem("oh_made")
        place = sem("place")
        idx_made = sem("idx_made")
        xg_in = sem("xg_in")
        x_t = sem("x_t")
        xet_made = sem("xet_made")
        gate_mm = sem("gate_mm")
        up_mm = sem("up_mm")
        g_exp = sem("g_exp")
        g_ln = sem("g_ln")
        g_sig = sem("g_sig")
        g_silu = sem("g_silu")
        hid = sem("hid")
        down_mm = sem("down_mm")
        yt_made = sem("yt_made")
        y_t = sem("y_t")
        ys_made = sem("ys_made")
        y_out = sem("y_out")
        added = sem("added")

        with nc.Block() as block:
            @block.sync
            def _(sp):
                sp.dma_start(mod_d[:, 3, :], MG[:]).then_inc(g2_out, 16)
                sp.wait_ge(g2_out, 16)
                for c in range(2):
                    sp.dma_start(G2[:, c], mod_d[c, 3].partition_broadcast(P)).then_inc(g2_in, 16)
                with sp.Fori(0, NE - 1) as e:
                    for slot in range(4, 12):
                        mm, c = (gate_mm, slot - 4) if slot < 8 else (up_mm, slot - 8)
                        sp.wait_ge(mm, e * KT + 2 * c + 2)
                        settled(sp)
                        expert_weights(sp, slot, e + 1)
                    for slot in range(4):
                        sp.wait_ge(down_mm, e * KT + 2 * slot + 2 + 1)
                        settled(sp)
                        expert_weights(sp, slot, e + 1)

            def fetch(pool, e, r):
                pool.wait_ge(idx_made, e + 1)
                if not isinstance(e, int):
                    pool.wait_ge(x_t, 3 * e)
                settled(pool)
                pool.indirect_dma_start(XG[:], None, h2_d, bass.IndirectOffsetOnAxis(IDX[:, 0, r:r + 1], 0)) \
                    .then_inc(xg_in, 16)
                pool.indirect_dma_start(XC[:], None, h2_d,
                                        bass.IndirectOffsetOnAxis(IDX[0:CAP_C, 1, r:r + 1], 0)) \
                    .then_inc(xg_in, 16)

            def add_rows(pool, e, r):
                pool.wait_ge(ys_made, e * 4 + 5)
                settled(pool)
                pool.indirect_dma_start(x1_d, bass.IndirectOffsetOnAxis(IDX[:, 0, r:r + 1], 0), YS[:], None,
                                        compute_op=ALU.add).then_inc(y_out, 16)
                pool.indirect_dma_start(x1_d, bass.IndirectOffsetOnAxis(IDX[0:CAP_C, 1, r:r + 1], 0), YC[:],
                                        None, compute_op=ALU.add).then_inc(y_out, 16)
                pool.wait_ge(y_out, e * 32 + 32)
                pool.sem_inc(added, 1)

            @block.gpsimd
            def _(pool):
                pool.sem_inc(added, 1)
                fetch(pool, 0, 0)
                with pool.Fori(0, NE // 2) as h:
                    for r in range(2):
                        e = 2 * h + r
                        fetch(pool, e + 1, 1 - r)
                        add_rows(pool, e, r)
                pool.wait_ge(xg_in, (NE + 1) * 32)

            @block.tensor
            def _(pe):
                def places(e):
                    pe.wait_ge(oh_made, e + 1)
                    if not isinstance(e, int):
                        pe.wait_ge(ys_made, e * 4 - 3)
                    for t in range(TL):
                        nc.tensor.matmul(PS[7][:, 0:2], OH[:, t, :], TA[:, t, ds(e, 1), :].rearrange("p a c -> p (a c)"),
                                         start=(t == 0), stop=(t == TL - 1))
                    nc.tensor.matmul(PS[7][0:CAP_C, 2:4], OH[:, CTX, 0:CAP_C],
                                     TA[:, CTX, ds(e, 1), :].rearrange("p a c -> p (a c)"),
                                     start=True, stop=True).then_inc(place, 1)

                def rows_t(e):
                    pe.wait_ge(xg_in, e * 32 + 32)
                    if not isinstance(e, int):
                        pe.wait_ge(xet_made, e * 3)
                        pe.wait_ge(ys_made, e * 4 - 3)
                    for h in range(2):
                        for k in range(4 * h, 4 * h + 4):
                            ins = nc.tensor.transpose(PS[4 + h][:, (k % 4) * P:(k % 4 + 1) * P],
                                                      XG[:, k * P:(k + 1) * P], IDENT)
                        ins.then_inc(x_t, 1)
                    for k in range(KT):
                        ins = nc.tensor.transpose(PS[6][:, k * CAP_C:(k + 1) * CAP_C], XC[:, k * P:(k + 1) * P],
                                                  IDENT[0:CAP_C, 0:CAP_C])
                    ins.then_inc(x_t, 1)

                def results_t(e, h):
                    pe.wait_ge(yt_made, e * KT + 4 * h + 4 + 1)
                    pe.wait_ge(idx_made, e + 2)
                    pe.wait_ge(xet_made, e * 3 + 6)
                    for q, (bank, rows) in enumerate(((7, slice(0, CAP_L)), (6, slice(CAP_L, NX)))):
                        n = rows.stop - rows.start
                        if h:
                            pe.wait_ge(ys_made, e * 4 + 1 + q + 1)
                        for f in range(4):
                            ins = nc.tensor.transpose(PS[bank][0:n, f * P:(f + 1) * P], YT[:, h, f, rows], IDENT)
                        ins.then_inc(y_t, 1)

                pe.sem_inc(y_t, 1)
                pe.sem_inc(down_mm, 1)
                places(0)
                rows_t(0)
                with pe.Fori(0, NE) as e:
                    for f in range(KT):
                        for s, mm in ((0, gate_mm), (1, up_mm)):
                            if f == 0:
                                if s == 0:
                                    pe.wait_ge(xet_made, e * 3 + 3)
                            if f % 2 == 0:
                                pe.wait_ge(we_in[4 + 4 * s + f // 2], e * 16 + 16)
                            if f < 2:
                                pe.wait_ge(yt_made, e * KT + 1)
                            elif s == 0:
                                pe.wait_ge(g_silu, e * KT + f)
                            else:
                                pe.wait_ge(hid, e * KT + f)
                            for k in range(KT):
                                ins = nc.tensor.matmul(PS[2 * s + f % 2][:, 0:NX],
                                                       WEA[:, 4 * s + f // 2, k, (f % 2) * P:(f % 2 + 1) * P],
                                                       XET[:, k, :], start=(k == 0), stop=(k == KT - 1))
                            ins.then_inc(mm, 1)
                        if f == 3:
                            places(e + 1)
                    rows_t(e + 1)
                    for f in range(KT):
                        if f % 2 == 0:
                            pe.wait_ge(we_in[f // 2], e * 16 + 16)
                        if f == 0:
                            pe.wait_ge(hid, e * KT + KT + 1)
                        if f >= 4:
                            pe.wait_ge(yt_made, e * KT + f - 2)
                        for k in range(KT):
                            ins = nc.tensor.matmul(PS[f % 4][:, 0:NX], WED[:, f // 2, k, (f % 2) * P:(f % 2 + 1) * P],
                                                   HID[:, k, :], start=(k == 0), stop=(k == KT - 1))
                        ins.then_inc(down_mm, 1)
                        if f == 5:
                            results_t(e, 0)
                    results_t(e, 1)

            @block.scalar
            def _(act):
                act.sem_inc(yt_made, 1)
                with act.Fori(0, NE) as e:
                    for f in range(KT):
                        n = e * KT + f
                        b = SG[:, f % 2]
                        act.wait_ge(gate_mm, n + 1)
                        act.wait_ge(g_silu, (e * KT + (f - 1 if f >= 2 else 0)) + 1)
                        nc.scalar.activation(b, PS[f % 2][:, 0:NX], ACT.Exp, scale=-1.0).then_inc(g_exp, 1)
                        act.wait_ge(g_exp, n + 1)
                        nc.scalar.activation(b, b, ACT.Ln, bias=1.0).then_inc(g_ln, 1)
                        act.wait_ge(g_ln, n + 1)
                        nc.scalar.activation(b, b, ACT.Exp, scale=-1.0).then_inc(g_sig, 1)
                    for f in range(KT):
                        act.wait_ge(down_mm, e * KT + f + 1 + 1)
                        act.wait_ge(y_t, e * 4 + 1)
                        nc.scalar.activation(YT[:, f // 4, f % 4], PS[f % 4][:, 0:NX], ACT.Copy).then_inc(yt_made, 1)

            @block.vector
            def _(dve):
                def one_hot(e):
                    if not isinstance(e, int):
                        dve.wait_ge(place, e)
                    for t in range(TN):
                        ins = nc.vector.tensor_scalar(OH[:, t], CST[:, C_IOTA:C_IOTA + P], POST[:, t, ds(e, 1)], None,
                                                      ALU.is_equal)
                    ins.then_inc(oh_made, 1)

                def places(e, r):
                    dve.wait_ge(place, e + 1)
                    if not isinstance(e, int):
                        dve.wait_ge(added, e)
                    nc.vector.tensor_copy(TW[:, 0, r:r + 1], PS[7][:, 1:2])
                    nc.vector.tensor_copy(TW[0:CAP_C, 1, r:r + 1], PS[7][0:CAP_C, 3:4])
                    nc.vector.tensor_copy(IDX[:, 0, r:r + 1], PS[7][:, 0:1])
                    nc.vector.tensor_copy(IDX[0:CAP_C, 1, r:r + 1], PS[7][0:CAP_C, 2:3]).then_inc(idx_made, 1)

                def rows(e):
                    dve.wait_ge(x_t, e * 3 + 1)
                    if not isinstance(e, int):
                        dve.wait_ge(up_mm, e * KT)
                    nc.vector.tensor_copy(XET[:, 0:4, 0:CAP_L], PS[4][:].rearrange("p (k n) -> p k n", k=4)) \
                      .then_inc(xet_made, 1)
                    dve.wait_ge(x_t, e * 3 + 2)
                    nc.vector.tensor_copy(XET[:, 4:8, 0:CAP_L], PS[5][:].rearrange("p (k n) -> p k n", k=4)) \
                      .then_inc(xet_made, 1)
                    dve.wait_ge(x_t, e * 3 + 3)
                    nc.vector.tensor_copy(XET[:, :, CAP_L:NX],
                                          PS[6][:, 0:KT * CAP_C].rearrange("p (k n) -> p k n", k=KT)) \
                      .then_inc(xet_made, 1)

                def results(e, h, r):
                    cols = slice(512 * h, 512 * h + 512)
                    for q, (bank, n, dst, c) in enumerate(((7, CAP_L, YS, 1), (6, CAP_C, YC, 0))):
                        dve.wait_ge(y_t, e * 4 + 2 * h + q + 1 + 1)
                        if h == 0 and q == 0:
                            dve.wait_ge(added, e + 1)
                        nc.vector.scalar_tensor_tensor(dst[0:n, cols], PS[bank][0:n, :], TW[0:n, q, r:r + 1],
                                                       G2[0:n, c, cols], ALU.mult, ALU.mult).then_inc(ys_made, 1)

                dve.sem_inc(ys_made, 1)
                dve.sem_inc(g_silu, 1)
                dve.sem_inc(hid, 1)
                one_hot(0)
                places(0, 0)
                rows(0)
                dve.wait_ge(g2_in, 32)
                with dve.Fori(0, NE // 2) as hh:
                    for r in range(2):
                        e = 2 * hh + r
                        one_hot(e + 1)
                        for f in range(KT):
                            n = e * KT + f
                            dve.wait_ge(g_sig, n + 1)
                            dve.wait_ge(hid, (n - 1 if f >= 1 else n) + 1)
                            nc.vector.tensor_tensor(GU[:, f % 2], SG[:, f % 2], PS[f % 2][:, 0:NX], ALU.mult) \
                              .then_inc(g_silu, 1)
                            dve.wait_ge(g_silu, n + 2)
                            dve.wait_ge(up_mm, n + 1)
                            if f == 0:
                                dve.wait_ge(down_mm, e * KT + 1)
                            nc.vector.tensor_tensor(HID[:, f], GU[:, f % 2], PS[2 + f % 2][:, 0:NX], ALU.mult) \
                              .then_inc(hid, 1)
                            if f == 5:
                                places(e + 1, 1 - r)
                        rows(e + 1)
                        for h in range(2):
                            results(e, h, r)

        next_stage()

        fn = Region(nc, after_w, hi)
        FN = fn("FN", [P, D])
        XF = fn("XF", [P, 4, D])
        YF = fn("YF", [P, 3, D])
        XJ3 = fn("XJ3", [P, D])
        RS3 = fn("RS3", [P, 2, TN])
        fn_in = sem("fn_in")
        xf_in = [sem(f"xf_in{i}") for i in range(4)]
        f_sq = sem("f_sq")
        f_ln = sem("f_ln")
        f_rs = sem("f_rs")
        f_out = sem("f_out")
        y_stored = [sem(f"y_stored{i}") for i in range(3)]
        y_rows = [y_sample[0, t * P:(t + 1) * P, :] for t in range(TL)] + [y_prompt[0]]

        with nc.Block() as block:
            @block.sync
            def _(sp):
                sp.dma_start(FN[:], final_norm.partition_broadcast(P)).then_inc(fn_in, 16)
                for t in range(TN):
                    if t >= 4:
                        sp.wait_ge(f_out, t - 3)
                    sp.dma_start(XF[:, t % 4], x1_d[t * P:(t + 1) * P, :]).then_inc(xf_in[t % 4], 16)

            @block.scalar
            def _(act):
                for t in range(TN):
                    act.wait_ge(xf_in[t % 4], 16 * (t // 4 + 1))
                    if t:
                        act.wait_ge(f_sq, t)
                    nc.scalar.activation(XJ3[:], XF[:, t % 4], ACT.Square,
                                         accum_out=RS3[:, 0, t:t + 1]).then_inc(f_sq, 1)
                    act.wait_ge(f_sq, t + 1)
                    nc.scalar.activation(RS3[:, 0, t:t + 1], RS3[:, 0, t:t + 1], ACT.Ln, bias=EPS,
                                         scale=1.0 / D).then_inc(f_ln, 1)
                    act.wait_ge(f_ln, t + 1)
                    nc.scalar.activation(RS3[:, 1, t:t + 1], RS3[:, 0, t:t + 1], ACT.Exp,
                                         scale=-0.5).then_inc(f_rs, 1)

            @block.vector
            def _(dve):
                dve.wait_ge(fn_in, 16)
                for t in range(TN):
                    dve.wait_ge(f_rs, t + 1)
                    if t >= 3:
                        dve.wait_ge(y_stored[t % 3], 16 * (t // 3))
                    nc.vector.scalar_tensor_tensor(YF[:, t % 3], XF[:, t % 4], RS3[:, 1, t:t + 1], FN[:],
                                                   ALU.mult, ALU.mult).then_inc(f_out, 1)

            @block.gpsimd
            def _(pool):
                for t in range(TN):
                    pool.wait_ge(f_out, t + 1)
                    pool.dma_start(y_rows[t], YF[:, t % 3]).then_inc(y_stored[t % 3], 16)
                for i in range(3):
                    pool.wait_ge(y_stored[i], 48)


_INS = ['x_prompt', 'x_sample', 'state_hgrn', 'c', 'c_ctx', 'w_ada', 'b_ada', 'norm1', 'w_in', 'conv_w', 'conv_b',
        'hgrn_lb', 'hgrn_onorm', 'w_out_a', 'w_out_b', 'w_o', 'norm2', 'w_router', 'w_e_gate', 'w_e_up',
        'w_e_down', 'final_norm']
_OUTS = [((1, P, D), 'float32'), ((1, TL * P, D), 'float32'), ((1, 1, 2, D // P, P, P), 'float32')]


def kernel(**inputs):
    import numpy as _np
    import concourse.bacc as _bacc
    from concourse import mybir as _mybir
    from concourse.bass_utils import run_bass_kernel_spmd as _run

    nc = _bacc.Bacc("TRN2", target_bir_lowering=False, num_devices=1)
    arrays = {f"in_{name}_dram": _np.ascontiguousarray(inputs[name]) for name in _INS}
    arrays["in_shape_constants_dram"] = shape_constants()
    args = [nc.dram_tensor(name, a.shape, _mybir.dt.from_np(a.dtype), kind="ExternalInput").ap()
            for name, a in arrays.items()]
    for i, (shape, dtype) in enumerate(_OUTS):
        dt = _mybir.dt.from_np(_np.dtype(dtype))
        args.append(nc.dram_tensor(f"out_{i}_dram", shape, dt, kind="ExternalOutput").ap())
    trunk(nc, *args)
    r = _run(nc, [arrays], core_ids=[0])
    return tuple(r.results[0][f"out_{i}_dram"] for i in range(len(_OUTS)))
```
